# Optimizing a Trainium2 kernel written in Bass

```python
import jax, jax.numpy as jnp
from jax import lax
import numpy as np

D_MODEL = 1024
BATCH = 1
SEQ = 512
DEPTH = 1

HGRN_HEADS = 4
HGRN_HEAD_DIM = 128
HGRN_WIDTH = HGRN_HEADS * HGRN_HEAD_DIM
HGRN_CHUNK = 64
FOX_HEADS = 8
FOX_HEAD_DIM = 64
FOX_WIDTH = FOX_HEADS * FOX_HEAD_DIM
FOX_QBLOCK = 128
PEER_HEADS = 8
PEER_DK = 256
PEER_DK_HALF = PEER_DK // 2
N_KEYS = 128
N_EXPERTS = N_KEYS * N_KEYS
PEER_TOPK = 16
PEER_CHUNK = 128

RMS_EPS = 1e-6

_IN_SIZES = (HGRN_WIDTH, HGRN_WIDTH, HGRN_WIDTH, HGRN_WIDTH,
             FOX_WIDTH, FOX_WIDTH, FOX_WIDTH, FOX_HEADS,
             D_MODEL, D_MODEL)
IN_WIDTH = sum(_IN_SIZES)
IN_SPLITS = tuple(int(v) for v in np.cumsum(_IN_SIZES)[:-1])

kernel_name = "hgrn2_fox_gated_peer_block"

def rms_norm(x, w):
    xf = x.astype(jnp.float32)
    y = xf * lax.rsqrt(jnp.mean(xf * xf, axis=-1, keepdims=True) + RMS_EPS)
    return (y * w.astype(jnp.float32)).astype(x.dtype)

def hgrn2_mixer(q, f_logit, i, g, lb, norm_w):
    B, S, _ = q.shape
    C, H, dh = HGRN_CHUNK, HGRN_HEADS, HGRN_HEAD_DIM
    n_chunks = S // C
    f32 = jnp.float32
    qf = jax.nn.silu(q.astype(f32))
    f = lb + (1.0 - lb) * jax.nn.sigmoid(f_logit.astype(f32))
    log_f = jnp.log(f)
    k = 1.0 - f

    def to_chunks(t):
        return t.reshape(B, n_chunks, C, H, dh).transpose(1, 0, 3, 2, 4)

    qc, kc, vc, lfc = to_chunks(qf), to_chunks(k), to_chunks(i.astype(f32)), to_chunks(log_f)
    causal = jnp.tril(jnp.ones((C, C), dtype=bool))

    def step(state, inp):
        qb, kb, vb, lfb = inp
        cum = jnp.cumsum(lfb, axis=-2)
        diff = cum[..., :, None, :] - cum[..., None, :, :]
        decay = jnp.exp(jnp.where(causal[:, :, None], diff, -jnp.inf))
        scores = jnp.einsum('bhtk,bhsk,bhtsk->bhts', qb, kb, decay)
        o = jnp.einsum('bhts,bhsv->bhtv', scores, vb) \
            + jnp.einsum('bhtk,bhkv->bhtv', qb * jnp.exp(cum), state)
        last = cum[..., -1:, :]
        new_state = jnp.exp(last[..., 0, :])[..., None] * state \
            + jnp.einsum('bhsk,bhsv->bhkv', kb * jnp.exp(last - cum), vb)
        return new_state, o

    s0 = jnp.zeros((B, H, dh, dh), f32)
    _, o = lax.scan(step, s0, (qc, kc, vc, lfc))
    o = o.transpose(1, 0, 3, 2, 4).reshape(B, S, H, dh)
    o = o * lax.rsqrt(jnp.mean(o * o, axis=-1, keepdims=True) + RMS_EPS)
    o = o * norm_w.astype(f32).reshape(H, dh)
    o = o.reshape(B, S, HGRN_WIDTH) * jax.nn.silu(g.astype(f32))
    return o.astype(q.dtype)

def fox_attention(q, k, v, f_logit, f_bias):
    B, S, _ = q.shape
    H, dh, QB = FOX_HEADS, FOX_HEAD_DIM, FOX_QBLOCK
    nb = S // QB
    log_f = jax.nn.log_sigmoid(f_logit.astype(jnp.float32) + f_bias.astype(jnp.float32))
    c = jnp.cumsum(log_f, axis=1).transpose(0, 2, 1)
    scale = dh ** -0.5
    qh = q.reshape(B, S, H, dh).transpose(0, 2, 1, 3) * scale
    kh = k.reshape(B, S, H, dh).transpose(0, 2, 1, 3)
    vh = v.reshape(B, S, H, dh).transpose(0, 2, 1, 3)
    q_blocks = qh.reshape(B, H, nb, QB, dh).transpose(2, 0, 1, 3, 4)
    cq_blocks = c.reshape(B, H, nb, QB).transpose(2, 0, 1, 3)
    key_pos = jnp.arange(S)

    def block(args):
        qb, cqb, bi = args
        s = jnp.einsum('bhqd,bhkd->bhqk', qb, kh).astype(jnp.float32)
        s = s + cqb[..., :, None] - c[..., None, :]
        q_pos = bi * QB + jnp.arange(QB)
        mask = key_pos[None, :] <= q_pos[:, None]
        p = jax.nn.softmax(jnp.where(mask, s, -jnp.inf), axis=-1)
        return jnp.einsum('bhqk,bhkd->bhqd', p.astype(vh.dtype), vh)

    o = lax.map(block, (q_blocks, cq_blocks, jnp.arange(nb)))
    return o.transpose(1, 0, 3, 2, 4).reshape(B, S, FOX_WIDTH)

def peer_ffn(x, w_q, sub_keys, u_table, v_table):
    B, S, D = x.shape
    T = B * S
    xt = x.reshape(T, D)
    q = (xt @ w_q).reshape(T, PEER_HEADS, 2, PEER_DK_HALF)
    s = jnp.einsum('thpd,hpnd->thpn', q, sub_keys).astype(jnp.float32)
    s1, i1 = lax.top_k(s[:, :, 0], PEER_TOPK)
    s2, i2 = lax.top_k(s[:, :, 1], PEER_TOPK)
    cand = (s1[..., :, None] + s2[..., None, :]).reshape(T, PEER_HEADS, PEER_TOPK * PEER_TOPK)
    cand_idx = (i1[..., :, None] * N_KEYS + i2[..., None, :]).reshape(T, PEER_HEADS, PEER_TOPK * PEER_TOPK)
    top_s, pos = lax.top_k(cand, PEER_TOPK)
    idx = jnp.take_along_axis(cand_idx, pos, axis=-1)
    gates = jax.nn.softmax(top_s, axis=-1).astype(x.dtype)
    nc = T // PEER_CHUNK
    HK = PEER_HEADS * PEER_TOPK

    def chunk(args):
        xc, ic, gc = args
        u = u_table[ic]
        a = jax.nn.gelu(jnp.einsum('cd,ced->ce', xc, u), approximate=False) * gc
        return jnp.einsum('ce,ced->cd', a, v_table[ic])

    out = lax.map(chunk, (xt.reshape(nc, PEER_CHUNK, D),
                          idx.reshape(nc, PEER_CHUNK, HK),
                          gates.reshape(nc, PEER_CHUNK, HK)))
    return out.reshape(B, S, D)

def setup_inputs(seed: int = 0) -> dict:
    key = jax.random.key(seed)
    ks = jax.random.split(key, 16)
    f32 = jnp.float32
    nrm = lambda k, shape, s: jax.random.normal(k, shape, f32) * s
    return {
        "x": nrm(ks[0], (BATCH, SEQ, D_MODEL), 1.0),
        "norm_mix_w": 1.0 + nrm(ks[1], (DEPTH, D_MODEL), 0.02),
        "w_in": nrm(ks[2], (DEPTH, D_MODEL, IN_WIDTH), D_MODEL ** -0.5),
        "hgrn_lb_logits": nrm(ks[3], (DEPTH + 1, HGRN_WIDTH), 0.5),
        "hgrn_norm_w": 1.0 + nrm(ks[4], (DEPTH, HGRN_WIDTH), 0.02),
        "fox_f_bias": 2.0 + nrm(ks[5], (DEPTH, FOX_HEADS), 0.5),
        "w_branch_hgrn": nrm(ks[6], (DEPTH, HGRN_WIDTH, D_MODEL), HGRN_WIDTH ** -0.5),
        "w_branch_fox": nrm(ks[7], (DEPTH, FOX_WIDTH, D_MODEL), FOX_WIDTH ** -0.5),
        "w_out": nrm(ks[8], (DEPTH, D_MODEL, D_MODEL), D_MODEL ** -0.5),
        "norm_ffn_w": 1.0 + nrm(ks[9], (DEPTH, D_MODEL), 0.02),
        "peer_w_q": nrm(ks[10], (DEPTH, D_MODEL, PEER_HEADS * PEER_DK), D_MODEL ** -0.5),
        "peer_sub_keys": nrm(ks[11], (DEPTH, PEER_HEADS, 2, N_KEYS, PEER_DK_HALF), PEER_DK_HALF ** -0.5),
        "peer_u": nrm(ks[12], (DEPTH, N_EXPERTS, D_MODEL), D_MODEL ** -0.5),
        "peer_v": nrm(ks[13], (DEPTH, N_EXPERTS, D_MODEL), 0.5),
        "norm_final_w": 1.0 + nrm(ks[14], (D_MODEL,), 0.02),
    }

def reference(x, norm_mix_w, w_in, hgrn_lb_logits, hgrn_norm_w, fox_f_bias, w_branch_hgrn,
              w_branch_fox, w_out, norm_ffn_w, peer_w_q, peer_sub_keys, peer_u, peer_v,
              norm_final_w):
    lb_all = jnp.cumsum(jax.nn.softmax(hgrn_lb_logits.astype(jnp.float32), axis=0), axis=0)
    h = x
    for l in range(DEPTH):
        xn = rms_norm(h, norm_mix_w[l])
        proj = xn @ w_in[l]
        hq, hf, hi, hg, fq, fk, fv, ff, ga, gb = jnp.split(proj, IN_SPLITS, axis=-1)
        a = hgrn2_mixer(hq, hf, hi, hg, lb_all[l], hgrn_norm_w[l])
        b = fox_attention(fq, fk, fv, ff, fox_f_bias[l])
        merged = jax.nn.sigmoid(ga) * (a @ w_branch_hgrn[l]) \
            + jax.nn.sigmoid(gb) * (b @ w_branch_fox[l])
        h = h + merged @ w_out[l]
        h = h + peer_ffn(rms_norm(h, norm_ffn_w[l]), peer_w_q[l], peer_sub_keys[l],
                         peer_u[l], peer_v[l])
    return rms_norm(h, norm_final_w)


_drawn_inputs = setup_inputs


def setup_inputs(seed=0):
    import zlib

    import numpy as np

    out = dict(_drawn_inputs(seed))
    spreads = {}
    factors = {'hgrn_norm_w': 3.012, 'norm_final_w': 2.874}
    for name, (base, spread) in spreads.items():
        noise = np.random.default_rng([zlib.crc32(name.encode()), seed]).standard_normal(out[name].shape)
        drawn = base * np.exp(spread * noise) if base else spread * noise
        out[name] = __import__('jax').numpy.asarray(drawn.astype(out[name].dtype))
    for name, factor in factors.items():
        out[name] = (out[name] * factor).astype(out[name].dtype)
    return out
```

```python
import concourse.bass as bass
from concourse import mybir
from contextlib import ExitStack

F32 = mybir.dt.float32
F32R = mybir.dt.float32r
BF16 = mybir.dt.bfloat16
U32 = mybir.dt.uint32
ALU = mybir.AluOpType
ACT = mybir.ActivationFunctionType
AX = mybir.AxisListType

P = 128
D = 1024
T = 512
KD = D // P
NT = T // P
HH, HF = 4, 8
DHF = 64
PH = 8
NK = 128
NC = NK
TOPK = 16
EPS = 1e-6
W = KD * P
LOWEST = -3.0e38

RAW, SPL = 4, 8
LEAD = 4
LOAD_LEAD = 7

COL_HF = [512 + P * i for i in range(4)]
COL_HQ = [P * i for i in range(4)]
COL_HI = [1024 + P * i for i in range(4)]
COL_FV = [3072 + P * i for i in range(4)]
COL_FF = [3584]
COL_FQ = [2048 + P * i for i in range(4)]
COL_FK = [2560 + P * i for i in range(4)]
COL_GATES = [3592 + P * i for i in range(16)]
COL_HG = [1536 + P * i for i in range(4)]
COLS = COL_HF + COL_HQ + COL_HI + COL_FV + COL_FF + COL_FQ + COL_FK + COL_GATES + COL_HG
N_IN = len(COLS)
HF0, HQ0, HI0, FV0, FF0, FQ0, FK0, GA0, HG0 = 0, 4, 8, 12, 16, 17, 21, 25, 41
BR0 = N_IN
WO0 = BR0 + KD
WQ0 = WO0 + KD
NQ = PH * 2
U0 = WQ0 + NQ
V0 = U0 + NC
N_UNITS = V0 + NC

LEVELS = 7
EV_DIAG, EV_OFFX, EV_OFFY, EV_OUT, EV = 7, 8, 9, 10, 11
HG_STEP0 = 12
FX_STEP0 = 26
PT_OFF = [0, 512, 896, 1152]
PT_LEN = [512, 384, 256, 128]
P_OFF = [0, 128, 384, 768]
TB = 32
QUAD = 4

TILE_LINKS = 154


def exp_events(e):
    return (e // EV) * 8 + min(e % EV, 7) + (1 if e % EV > EV_OFFX else 0)


def hgrn_slots(n):
    lo = 2 * (n - HG_STEP0)
    return [e for e in (lo, lo + 1) if 0 <= e < EV * HH]


def exp_slot(e):
    return ((e // EV) * LEVELS + e % EV) % 3


def build(nc, xT, w_in, norm_mix, lb_logits, hgrn_norm, fox_bias, w_a, w_b, w_out, norm_ffn, w_q, keys,
          u_t, v_tab, norm_final, c_f32, c_mask, c_iota, yT):
    gates_d = nc.dram_tensor("gates_raw", (16, P, T), F32, kind="Internal").ap()
    scores_d = nc.dram_tensor("key_scores", (NT, P, NQ, NK), F32, kind="Internal").ap()
    gelu_d = nc.dram_tensor("gelu_ux", (NC, P, T), F32, kind="Internal").ap()
    dense_d = nc.dram_tensor("dense_gates", (T // TB, P, NC * TB), F32, kind="Internal").ap()

    outer = ExitStack()

    def sb(ctx, name, shape, dt=F32):
        return ctx.enter_context(nc.sbuf_tensor(name, shape, dt))

    def sem(name):
        return outer.enter_context(nc.semaphore(name))

    with outer:
        raw = sb(outer, "raw", [P, RAW, W])
        spl = sb(outer, "spl", [P, 2, SPL, W], F32R)
        act = sb(outer, "act", [P, 2, KD, T], F32R)
        ab = sb(outer, "ab", [P, KD, T])
        cst = sb(outer, "cst", [P, 3, P])
        nrm = sb(outer, "nrm", [P, 3, KD])
        ident, cmask, ones = cst[:, 0, :], cst[:, 1, :], cst[:, 2, :]
        bank = [outer.enter_context(nc.psum_tensor(f"bank{i}", [P, T], F32)) for i in range(8)]

        unit_loaded = [sem(f"unit_loaded{i}") for i in range(RAW)]
        hi_done, lo_done, unit_used = sem("hi_done"), sem("lo_done"), sem("unit_used")

        def unit_source(n):
            if n < BR0:
                return w_in[:, COLS[n]:COLS[n] + P].rearrange("(k p) c -> p k c", p=P)
            if n < WO0:
                return None
            if n < WQ0:
                c = (n - WO0) * P
                return w_out[:, c:c + P].rearrange("(k p) c -> p k c", p=P)
            if n < U0:
                c = (n - WQ0) * P
                return w_q[:, c:c + P].rearrange("(k p) c -> p k c", p=P)
            if n < V0:
                return u_t[n - U0, :, :]
            return v_tab[:, n - V0, :]

        def load_unit(sp, n):
            if n >= RAW:
                sp.wait_ge(lo_done, n - RAW + 1)
            s = n % RAW
            if BR0 <= n < WO0:
                c = (n - BR0) * P
                dst = raw[:, s, :].rearrange("p (k c) -> p k c", k=KD)
                sp.dma_start(dst[:, 0:4, :], w_a[:, c:c + P].rearrange("(k p) c -> p k c", p=P)) \
                    .then_inc(unit_loaded[s], 16)
                sp.dma_start(dst[:, 4:8, :], w_b[:, c:c + P].rearrange("(k p) c -> p k c", p=P)) \
                    .then_inc(unit_loaded[s], 16)
            elif n < U0:
                sp.dma_start(raw[:, s, :].rearrange("p (k c) -> p k c", k=KD), unit_source(n)) \
                    .then_inc(unit_loaded[s], 16)
            else:
                sp.dma_start(raw[:, s, :], unit_source(n)).then_inc(unit_loaded[s], 16)

        def loads_before(n, s):
            return sum(2 if BR0 <= m < WO0 else 1 for m in range(s, n + 1, RAW))

        def last_step(n):
            return n | 3 if HI0 <= n < FF0 else n

        def split_hi(eng, n, group=None):
            s = n % RAW
            extra = 0 if group is None else group * (16 // RAW)
            more = 0 if group is None else group
            eng.wait_ge(unit_loaded[s], extra + 16 * loads_before(n, s))
            if n >= SPL:
                eng.wait_ge(unit_used, more + last_step(n - SPL) + 1)
            eng.activation(spl[:, 0, n % SPL, :], raw[:, s, :], ACT.Copy).then_inc(hi_done, 1)

        def split_lo(eng, n, group=None):
            more = 0 if group is None else group
            eng.wait_ge(hi_done, more + n + 1)
            eng.tensor_tensor(spl[:, 1, n % SPL, :], raw[:, n % RAW, :],
                              spl[:, 0, n % SPL, :].bitcast(F32), ALU.subtract).then_inc(lo_done, 1)

        def passes(out, w_hi, w_lo, x_hi, x_lo, first, last):
            nc.tensor.matmul(out, w_hi, x_hi, start=first, stop=False)
            nc.tensor.matmul(out, w_hi, x_lo, start=False, stop=False)
            return nc.tensor.matmul(out, w_lo, x_hi, start=False, stop=last)

        def unit_product(out, n, src):
            for k in range(KD):
                c = slice(k * P, (k + 1) * P)
                ins = passes(out, spl[:, 0, n % SPL, c], spl[:, 1, n % SPL, c],
                             src[:, 0, k, :], src[:, 1, k, :], k == 0, k == KD - 1)
            return ins

        ctx = ExitStack()
        with ctx:
            kc = sb(ctx, "kc", [P, 8, T])
            late = sb(ctx, "late", [P, KD, T])
            fk = sb(ctx, "fk", [P, 4, T])
            lev = sb(ctx, "lev", [P, 3, T])
            s_diag = sb(ctx, "s_diag", [P, NT, P])
            s_off = sb(ctx, "s_off", [P, 6, P])
            off_q = sb(ctx, "off_q", [P, 4, P])
            off_k = sb(ctx, "off_k", [P, 4, P])
            etot = sb(ctx, "etot", [P, 2])
            masks = sb(ctx, "masks", [P, 8, P], mybir.dt.uint8)
            head_row = sb(ctx, "head_row", [HF, HF, P])
            negc = sb(ctx, "negc", [HF, T])
            probs = sb(ctx, "probs", [P, 1280])
            probs_t = sb(ctx, "probs_t", [P, 1280])
            stat = sb(ctx, "stat", [P, 4, 4])
            spill = sb(ctx, "spill", [P, 2, T])
            lbt = sb(ctx, "lbt", [P, 8, 4])
            hnw = sb(ctx, "hnw", [P, 4])
            fbias = sb(ctx, "fbias", [HF, 1])
            ones_row = sb(ctx, "ones_row", [P, P])
            ff = probs[0:HF, 0:2 * T].rearrange("p (a t) -> p a t", a=2)
            hv, fv = late[:, 0:4, :], late[:, 4:8, :]
            kk, cum = kc[:, 0:4, :], kc[:, 4:8, :]

            consts_in, mask_in, x_in, small_in = sem("consts_in"), sem("mask_in"), sem("x_in"), sem("small_in")
            lb_diff, lb_exp = sem("lb_diff"), sem("lb_exp")
            squares, mean_mm, mean_ready, root_ready = sem("squares"), sem("mean_mm"), sem("mean_ready"), \
                sem("root_ready")
            xn_ready, xn_hi, xn_lo = sem("xn_ready"), sem("xn_hi"), sem("xn_lo")
            chain = sem("chain")
            achain = sem("achain")
            proj_out = [sem("proj_out0"), sem("proj_out1")]
            sig_ready, pool_zero, f_scan = sem("sig_ready"), sem("pool_zero"), sem("f_scan")
            f_ready, logf_ready = sem("f_ready"), sem("logf_ready")
            spilled = [sem("spilled0"), sem("spilled1")]
            ff_abs, ff_soft, c_ready = sem("ff_abs"), sem("ff_soft"), sem("c_ready")
            hg_diff, hg_exp, hg_pre, hg_mm, hg_post = sem("hg_diff"), sem("hg_exp"), sem("hg_pre"), \
                sem("hg_mm"), sem("hg_post")
            fx_score, fx_max, fx_exp, fx_norm, fx_tr, fx_trout, fx_pv, fx_out = (
                sem("fx_score"), sem("fx_max"), sem("fx_exp"), sem("fx_norm"), sem("fx_tr"),
                sem("fx_trout"), sem("fx_pv"), sem("fx_out"))
            on_sq, on_mm, on_mean, on_root = sem("on_sq"), sem("on_mm"), sem("on_mean"), sem("on_root")

            block = ctx.enter_context(nc.Block())

            def level_view(buf, h_size):
                return buf.rearrange("p (b u x) -> p b u x", u=2, x=h_size)

            @block.sync
            def _(sp):
                xv = xT.rearrange("(k p) t -> p k t", p=P)
                sp.dma_start(late[:, 0:4, :], xv[:, 0:4, :]).then_inc(x_in, 16)
                sp.dma_start(late[:, 4:8, :], xv[:, 4:8, :]).then_inc(x_in, 16)
                sp.dma_start(cst[:, :, :], c_f32).then_inc(consts_in, 16)
                sp.dma_start(nrm[:, 0, :], norm_mix).then_inc(small_in, 16)
                sp.dma_start(lbt[:, 0:2, :], lb_logits).then_inc(small_in, 16)
                sp.dma_start(nrm[:, 1, :], norm_ffn).then_inc(small_in, 16)
                sp.dma_start(nrm[:, 2, :], norm_final).then_inc(small_in, 16)
                sp.dma_start(hnw[:, :], hgrn_norm).then_inc(small_in, 16)
                sp.dma_start(fbias[:, :], fox_bias).then_inc(small_in, 16)
                sp.dma_start(probs[:, 0:8 * P], c_mask).then_inc(mask_in, 16)
                for n in range(LOAD_LEAD):
                    load_unit(sp, n)
                for n in range(N_IN):
                    load_unit(sp, n + LOAD_LEAD)
                    g = n - GA0 - 1
                    if 0 <= g < 16:
                        sp.wait_ge(proj_out[(n - 1) % 2], (n - 1) // 2 + 1)
                        sp.dma_start(gates_d[g, :, :], spill[:, g % 2, :]).then_inc(spilled[g % 2], 16)
                for s in range(2):
                    sp.wait_ge(spilled[s], 16 * 8)

            @block.gpsimd
            def _(pool):
                pool.memset(s_diag[:, :, :], 0.0).then_inc(pool_zero, 1)
                pool.memset(ones_row[:, :], 1.0).then_inc(pool_zero, 1)
                pool.wait_ge(mask_in, 16)
                pool.tensor_copy(masks[:, :, :].rearrange("p l t -> p (l t)"), probs[:, 0:8 * P]) \
                    .then_inc(pool_zero, 1)
                for n in range(LEAD):
                    split_lo(pool, n)
                for n in range(N_IN):
                    split_lo(pool, n + LEAD)

            def act_fox_exp(act_e, h):
                for i in (3, 2, 1, 0):
                    act_e.wait_ge(fx_max, 4 * h + (4 - i if i > 1 else 4))
                    if h >= 1 and i == 3:
                        act_e.wait_ge(fx_tr, 4 * h)
                    act_e.activation(probs[:, P_OFF[i]:P_OFF[i] + (i + 1) * P], fox_scores(i), ACT.Exp,
                                     bias=stat[:, 0, i:i + 1],
                                     accum_out=stat[:, 1, i:i + 1]).then_inc(fx_exp, 1)

            def fox_scores(i):
                if i == 3:
                    return bank[4][:, :]
                if i == 2:
                    return bank[5][:, 0:384]
                return bank[6][:, 0:256] if i == 1 else bank[6][:, 256:384]

            def fox_tr_bank(j):
                return bank[[7, 4, 5, 6][j]][:, 0:PT_LEN[j]]

            def hgrn_exp(act_e, e):
                if e >= EV * HH:
                    return
                h, l = divmod(e, EV)
                if l < LEVELS:
                    b = exp_slot(e)
                    act_e.wait_ge(hg_diff, h * LEVELS + l + 1)
                    act_e.activation(lev[:, b, :], lev[:, b, :], ACT.Exp).then_inc(hg_exp, 1)
                elif l == EV_OFFX:
                    if h == 0:
                        act_e.wait_ge(f_scan, HH)
                    if h >= 1:
                        act_e.wait_ge(hg_mm, EV * (h - 1) + EV_OFFY + 1)
                    c = cum[:, h, :].rearrange("p (i x) -> p i x", i=NT)
                    act_e.activation(off_q[:, 0:2, :], c[:, 1:3, :], ACT.Exp)
                    act_e.activation(off_q[:, 3, :], c[:, 3, :], ACT.Exp)
                    for i, slot in ((0, 3), (1, 1), (2, 2)):
                        act_e.activation(off_k[:, slot, :], c[:, i, :], ACT.Exp,
                                         bias=c[:, i, P - 1:P], scale=-1.0)
                    act_e.activation(etot[:, 0:2], c[:, 1:3, P - 1], ACT.Exp).then_inc(hg_exp, 1)

            @block.scalar
            def _(act_e):
                for n in range(LEAD):
                    split_hi(act_e, n)
                for k in range(KD):
                    act_e.wait_ge(x_in, 32)
                    act_e.activation(kc[:, k, :], late[:, k, :], ACT.Square).then_inc(squares, 1)
                act_e.wait_ge(mean_ready, 1)
                act_e.activation(lev[:, 1, :], lev[:, 0, :], ACT.Sqrt).then_inc(root_ready, 1)
                for k in range(KD):
                    act_e.wait_ge(xn_ready, k + 1)
                    act_e.activation(act[:, 0, k, :], late[:, k, :], ACT.Copy).then_inc(xn_hi, 1)
                act_e.wait_ge(lb_diff, 1)
                act_e.activation(lbt[:, 2:4, :], lbt[:, 2:4, :], ACT.Exp).then_inc(lb_exp, 1)

                for n in range(N_IN):
                    split_hi(act_e, n + LEAD)
                    pr = bank[n % 2]
                    act_e.wait_ge(unit_used, n + 1)
                    if n < HQ0:
                        act_e.activation(kk[:, n, :], pr[:, :], ACT.Sigmoid).then_inc(proj_out[n % 2], 1)
                    elif n < HI0:
                        if n - HQ0 >= 2:
                            act_e.wait_ge(proj_out[n % 2], n // 2)
                        act_e.activation(lev[:, n % 2, :], pr[:, :], ACT.Sigmoid).then_inc(sig_ready, 1)
                    elif n < FV0:
                        act_e.activation(hv[:, n - HI0, :], pr[:, :], ACT.Copy).then_inc(proj_out[n % 2], 1)
                    elif n < FF0:
                        act_e.activation(fv[:, n - FV0, :], pr[:, :], ACT.Copy).then_inc(proj_out[n % 2], 1)
                    elif n == FF0:
                        act_e.wait_ge(ff_abs, 1)
                        act_e.activation(ff[:, 1, :], ff[:, 1, :], ACT.Exp).then_inc(achain, 1)
                        act_e.wait_ge(achain, 1)
                        act_e.activation(ff[:, 1, :], ff[:, 1, :], ACT.Ln, bias=1.0).then_inc(ff_soft, 1)
                    elif n < FK0:
                        act_e.activation(ab[:, 4 + n - FQ0, :], pr[:, :], ACT.Copy,
                                         scale=DHF ** -0.5).then_inc(proj_out[n % 2], 1)
                    elif n < GA0:
                        act_e.activation(fk[:, n - FK0, :], pr[:, :], ACT.Copy).then_inc(proj_out[n % 2], 1)
                    elif n < HG0:
                        g = n - GA0
                        if g >= 2:
                            act_e.wait_ge(spilled[g % 2], 16 * (g // 2))
                        act_e.activation(spill[:, g % 2, :], pr[:, :], ACT.Copy).then_inc(proj_out[n % 2], 1)
                    else:
                        if n - HG0 >= 2:
                            act_e.wait_ge(proj_out[n % 2], n // 2)
                        act_e.activation(lev[:, n % 2, :], pr[:, :], ACT.Sigmoid).then_inc(sig_ready, 1)
                    if n == HI0 - 1:
                        for h in range(HH):
                            act_e.wait_ge(f_ready, h + 1)
                            act_e.activation(cum[:, h, :], cum[:, h, :], ACT.Ln).then_inc(logf_ready, 1)
                    if n == HG_STEP0 - 1:
                        hgrn_exp(act_e, 0)
                        hgrn_exp(act_e, 1)
                    for e in hgrn_slots(n):
                        hgrn_exp(act_e, e + 2)
                    h = n - FX_STEP0
                    if 0 <= h < 2 * HF:
                        if h % 2 == 0:
                            act_fox_exp(act_e, h // 2)
                        else:
                            for j in range(4):
                                act_e.wait_ge(fx_tr, 4 * (h // 2) + j + 1)
                                if h >= 2 and j == 0:
                                    act_e.wait_ge(fx_pv, h // 2)
                                act_e.activation(probs_t[:, PT_OFF[j]:PT_OFF[j] + PT_LEN[j]],
                                                 fox_tr_bank(j), ACT.Copy).then_inc(fx_trout, 1)
                    if n == 34:
                        for h in range(HH):
                            act_e.wait_ge(hg_post, EV * (h + 1))
                            act_e.activation(kk[:, h, :], ab[:, h, :], ACT.Square).then_inc(on_sq, 1)
                    if n == 36:
                        for h in range(HH):
                            act_e.wait_ge(on_mean, h + 1)
                            act_e.activation(cum[:, h, :], cum[:, h, :], ACT.Sqrt).then_inc(on_root, 1)

            @block.vector
            def _(dve):
                steps = [0]

                def link(ins):
                    steps[0] += 1
                    ins.then_inc(chain, 1)
                    dve.wait_ge(chain, steps[0])

                dve.wait_ge(small_in, 16 * 6)
                link(dve.tensor_tensor(lbt[:, 4, :], lbt[:, 0, :], lbt[:, 1, :], ALU.max))
                link(dve.tensor_tensor(lbt[:, 2, :], lbt[:, 0, :], lbt[:, 4, :], ALU.subtract))
                dve.tensor_tensor(lbt[:, 3, :], lbt[:, 1, :], lbt[:, 4, :], ALU.subtract).then_inc(lb_diff, 1)
                dve.wait_ge(mean_mm, 1)
                dve.tensor_scalar(lev[:, 0, :], bank[4][:, :], 1.0 / D, EPS, ALU.mult, ALU.add) \
                    .then_inc(mean_ready, 1)
                dve.wait_ge(root_ready, 1)
                link(dve.reciprocal(lev[:, 2, :], lev[:, 1, :]))
                for k in range(KD):
                    dve.scalar_tensor_tensor(out=late[:, k, :], in0=late[:, k, :], scalar=nrm[:, 0, k:k + 1],
                                             in1=lev[:, 2, :], op0=ALU.mult, op1=ALU.mult) \
                        .then_inc(xn_ready, 1)
                    if k >= 1:
                        dve.wait_ge(xn_hi, k)
                        dve.tensor_tensor(act[:, 1, k - 1, :], late[:, k - 1, :],
                                          act[:, 0, k - 1, :].bitcast(F32), ALU.subtract).then_inc(xn_lo, 1)
                dve.wait_ge(xn_hi, KD)
                dve.tensor_tensor(act[:, 1, KD - 1, :], late[:, KD - 1, :],
                                  act[:, 0, KD - 1, :].bitcast(F32), ALU.subtract).then_inc(xn_lo, 1)
                dve.wait_ge(lb_exp, 1)
                link(dve.tensor_tensor(lbt[:, 5, :], lbt[:, 2, :], lbt[:, 3, :], ALU.add))
                link(dve.reciprocal(lbt[:, 6, :], lbt[:, 5, :]))
                link(dve.tensor_tensor(lbt[:, 4, :], lbt[:, 2, :], lbt[:, 6, :], ALU.mult))
                link(dve.tensor_scalar(lbt[:, 5, :], lbt[:, 4, :], -1.0, 1.0, ALU.mult, ALU.add))
                link(dve.tensor_scalar(lbt[:, 6, :], lbt[:, 5, :], -1.0, None, ALU.mult))

                def pre1(e):
                    if e >= EV * HH or e % EV >= LEVELS:
                        return
                    h, l = divmod(e, EV)
                    hs = 64 >> l
                    c = level_view(cum[:, h, :], hs)
                    o = level_view(lev[:, exp_slot(e), :], hs)
                    mid = c[:, :, 0, hs - 1:hs].to_broadcast([P, T // (2 * hs), hs])
                    dve.tensor_tensor(o[:, :, 1, :], c[:, :, 1, :], mid, ALU.subtract)
                    dve.tensor_tensor(o[:, :, 0, :], mid, c[:, :, 0, :], ALU.subtract).then_inc(hg_diff, 1)

                def pre2(e):
                    if e >= EV * HH:
                        return
                    h, l = divmod(e, EV)
                    if l < LEVELS:
                        hs = 64 >> l
                        o = level_view(lev[:, exp_slot(e), :], hs)
                        q = level_view(ab[:, h, :], hs)
                        k = level_view(kk[:, h, :], hs)
                        dve.wait_ge(hg_exp, exp_events(e) + 1)
                        dve.tensor_tensor(o[:, :, 1, :], o[:, :, 1, :], q[:, :, 1, :], ALU.mult)
                        dve.tensor_tensor(o[:, :, 0, :], o[:, :, 0, :], k[:, :, 0, :], ALU.mult) \
                            .then_inc(hg_pre, 1)
                    elif l == EV_OFFX:
                        q = ab[:, h, :].rearrange("p (i x) -> p i x", i=NT)
                        k = kk[:, h, :].rearrange("p (i x) -> p i x", i=NT)
                        dve.wait_ge(hg_exp, exp_events(e) + 1)
                        dve.tensor_tensor(off_q[:, 0:2, :], off_q[:, 0:2, :], q[:, 1:3, :], ALU.mult)
                        dve.tensor_tensor(off_q[:, 3, :], off_q[:, 3, :], q[:, 3, :], ALU.mult)
                        dve.tensor_tensor(off_k[:, 1:3, :], off_k[:, 1:3, :], k[:, 1:3, :], ALU.mult)
                        link(dve.tensor_tensor(off_k[:, 3, :], off_k[:, 3, :], k[:, 0, :], ALU.mult))
                        dve.tensor_scalar(off_q[:, 2, :], off_q[:, 3, :], etot[:, 1:2], None, ALU.mult)
                        dve.tensor_scalar(off_k[:, 0, :], off_k[:, 3, :], etot[:, 0:1], None, ALU.mult) \
                            .then_inc(hg_pre, 1)

                def post(e):
                    h, l = divmod(e, EV)
                    b = bank[2 + e % 2]
                    dve.wait_ge(hg_mm, e + 1)
                    if l <= EV_DIAG:
                        if e >= 1:
                            dve.wait_ge(hg_post, e)
                        ins = dve.copy_predicated(s_diag[:, :, :],
                                                  masks[:, l:l + 1, :].to_broadcast([P, NT, P]),
                                                  b[:, :].rearrange("p (i x) -> p i x", i=NT))
                    elif l == EV_OFFX:
                        ins = dve.tensor_copy(s_off[:, 0:4, :], b[:, :].rearrange("p (i x) -> p i x", i=NT))
                    elif l == EV_OFFY:
                        ins = dve.tensor_copy(s_off[:, 4:6, :],
                                              b[:, 0:2 * P].rearrange("p (i x) -> p i x", i=2))
                    else:
                        ins = dve.tensor_copy(ab[:, h, :], b[:, :])
                    ins.then_inc(hg_post, 1)

                def fox_norm(h):
                    dve.wait_ge(fx_score, h + 1)
                    for i in (3, 2, 1, 0):
                        dve.tensor_reduce(stat[:, 0, i:i + 1], fox_scores(i), AX.X, ALU.max, negate=True) \
                            .then_inc(fx_max, 1)
                    for i in (3, 2, 1, 0):
                        dve.wait_ge(fx_exp, 4 * h + 4 - i)
                        link(dve.reciprocal(stat[:, 2, i:i + 1], stat[:, 1, i:i + 1]))
                        p = probs[:, P_OFF[i]:P_OFF[i] + (i + 1) * P]
                        dve.tensor_scalar(p, p, stat[:, 2, i:i + 1], None, ALU.mult).then_inc(fx_norm, 1)

                def fox_out(h):
                    p0 = DHF * (h % 2)
                    dve.wait_ge(fx_pv, h + 1)
                    dve.tensor_copy(ab[p0:p0 + DHF, 4 + h // 2, :], bank[7][0:DHF, :]).then_inc(fx_out, 1)

                for n in range(N_IN):
                    pr = bank[n % 2]
                    if n < HQ0:
                        dve.wait_ge(proj_out[n % 2], n // 2 + 1)
                        dve.tensor_scalar(cum[:, n, :], kk[:, n, :], lbt[:, 5, n:n + 1], lbt[:, 4, n:n + 1],
                                          ALU.mult, ALU.add).then_inc(f_ready, 1)
                        dve.tensor_scalar(kk[:, n, :], kk[:, n, :], lbt[:, 6, n:n + 1], lbt[:, 5, n:n + 1],
                                          ALU.mult, ALU.add)
                    elif n < HI0:
                        dve.wait_ge(sig_ready, n - HQ0 + 1)
                        dve.tensor_tensor(ab[:, n - HQ0, :], pr[:, :], lev[:, n % 2, :], ALU.mult) \
                            .then_inc(proj_out[n % 2], 1)
                    if n == HI0 - 1:
                        dve.wait_ge(pool_zero, 3)
                        for h in range(HH):
                            dve.wait_ge(logf_ready, h + 1)
                            for i in range(NT):
                                c = cum[:, h, i * P:(i + 1) * P]
                                ins = dve.tensor_tensor_scan(c, ones_row[:, :], c, 0.0, ALU.mult, ALU.add)
                            ins.then_inc(f_scan, 1)
                        dve.wait_ge(f_scan, HH)
                    if n == FF0:
                        dve.wait_ge(unit_used, n + 1)
                        dve.tensor_scalar(ff[:, 0, :], pr[0:HF, :], fbias[:, 0:1], None, ALU.add) \
                            .then_inc(proj_out[n % 2], 1)
                        dve.wait_ge(proj_out[n % 2], n // 2 + 1)
                        dve.scalar_tensor_tensor(out=ff[:, 1, :], in0=ff[:, 0, :], scalar=-1.0,
                                                 in1=ff[:, 0, :], op0=ALU.mult, op1=ALU.max)
                        link(dve.tensor_scalar(negc[:, :], ff[:, 0, :], 0.0, None, ALU.min))
                        dve.tensor_scalar(ff[:, 1, :], ff[:, 1, :], -1.0, None, ALU.mult).then_inc(ff_abs, 1)
                        dve.wait_ge(ff_soft, 1)
                        link(dve.tensor_tensor(ff[:, 0, :], negc[:, :], ff[:, 1, :], ALU.subtract))
                        dve.memset(ff[:, 1, :], 1.0)
                        for h in range(HF):
                            ins = dve.tensor_copy(head_row[:, h, :],
                                                  ident[0:HF, h:h + 1].to_broadcast([HF, P]))
                        link(ins)
                        dve.tensor_tensor_scan(negc[:, :], ff[:, 1, :], ff[:, 0, :], 0.0,
                                               ALU.mult, ALU.subtract).then_inc(c_ready, 1)
                    if n == HG_STEP0 - 1:
                        pre1(0)
                        pre1(1)
                        pre2(0)
                    for e in hgrn_slots(n):
                        pre2(e + 1)
                        pre1(e + 2)
                        post(e)
                    h = n - FX_STEP0
                    if 0 <= h <= 2 * HF and h % 2 == 0:
                        if h >= 2:
                            fox_out(h // 2 - 1)
                        if h < 2 * HF:
                            fox_norm(h // 2)
                    if n == 35:
                        for h in range(HH):
                            dve.wait_ge(on_mm, h + 1)
                            dve.tensor_scalar(cum[:, h, :], bank[2 + h % 2][:, :], 1.0 / P, EPS,
                                              ALU.mult, ALU.add).then_inc(on_mean, 1)
                    if 37 <= n < 41:
                        h = n - 37
                        dve.wait_ge(on_root, h + 1)
                        link(dve.reciprocal(cum[:, h, :], cum[:, h, :]))
                        link(dve.scalar_tensor_tensor(out=ab[:, h, :], in0=ab[:, h, :],
                                                      scalar=hnw[:, h:h + 1], in1=cum[:, h, :],
                                                      op0=ALU.mult, op1=ALU.mult))
                    if n >= HG0:
                        h = n - HG0
                        dve.wait_ge(sig_ready, 4 + h + 1)
                        link(dve.tensor_tensor(lev[:, n % 2, :], pr[:, :], lev[:, n % 2, :], ALU.mult))
                        dve.tensor_tensor(ab[:, h, :], ab[:, h, :], lev[:, n % 2, :], ALU.mult) \
                            .then_inc(proj_out[n % 2], 1)

            @block.tensor
            def _(pe):
                pe.wait_ge(consts_in, 16)
                for k in range(KD):
                    pe.wait_ge(squares, k + 1)
                    ins = nc.tensor.matmul(bank[4][:, :], ones, kc[:, k, :], start=k == 0, stop=k == KD - 1)
                ins.then_inc(mean_mm, 1)
                pe.wait_ge(xn_lo, KD)

                def project(n):
                    pe.wait_ge(lo_done, last_step(n) + 1)
                    if n >= 2:
                        pe.wait_ge(proj_out[n % 2], n // 2)
                    out = bank[n % 2][:, :]
                    if HI0 <= n < FF0:
                        i, s0 = n % 4, (n & ~3) % SPL
                        t = slice(i * P, (i + 1) * P)
                        for k in range(KD):
                            c = slice(k * P, (k + 1) * P)
                            ins = passes(out, act[:, 0, k, t], act[:, 1, k, t], spl[:, 0, s0:s0 + 4, c],
                                         spl[:, 1, s0:s0 + 4, c], k == 0, k == KD - 1)
                    else:
                        ins = unit_product(out, n, act)
                    ins.then_inc(unit_used, 1)

                def hgrn_mm(e):
                    h, l = divmod(e, EV)
                    b = bank[2 + e % 2]
                    if e >= 2:
                        pe.wait_ge(hg_post, e - 1)
                    hs = slice(h * P, (h + 1) * P)
                    if l < LEVELS:
                        pe.wait_ge(hg_pre, exp_events(e) + 1)
                        f = lev[:, exp_slot(e), :]
                        for i in range(NT):
                            c = slice(i * P, (i + 1) * P)
                            ins = nc.tensor.matmul(b[:, c], f[:, c], f[:, c], start=True, stop=True)
                    elif l == EV_DIAG:
                        for i in range(NT):
                            c = slice(i * P, (i + 1) * P)
                            ins = nc.tensor.matmul(b[:, c], kk[:, h, c], ab[:, h, c], start=True, stop=True)
                    elif l == EV_OFFX:
                        pe.wait_ge(hg_pre, exp_events(e) + 1)
                        for cols, s, q in ((slice(0, P), 3, slice(0, 1)), (slice(P, 3 * P), 0, slice(1, 3)),
                                           (slice(3 * P, T), 2, slice(3, 4))):
                            ins = nc.tensor.matmul(b[:, cols], off_k[:, s, :], off_q[:, q, :],
                                                   start=True, stop=True)
                    elif l == EV_OFFY:
                        ins = nc.tensor.matmul(b[:, 0:2 * P], off_k[:, 1, :], off_q[:, 1:3, :],
                                               start=True, stop=True)
                    else:
                        pe.wait_ge(hg_post, e)
                        nc.tensor.matmul(b[:, 0:P], hv[:, 0, hs], s_diag[:, 0, :], start=True, stop=False)
                        nc.tensor.matmul(b[:, P:T], hv[:, 0, hs], s_off[:, 0:3, :], start=False, stop=False)
                        nc.tensor.matmul(b[:, P:2 * P], hv[:, 1, hs], s_diag[:, 1, :], start=False, stop=False)
                        nc.tensor.matmul(b[:, 2 * P:T], hv[:, 1, hs], s_off[:, 4:6, :], start=False, stop=False)
                        nc.tensor.matmul(b[:, 2 * P:3 * P], hv[:, 2, hs], s_diag[:, 2, :],
                                         start=False, stop=False)
                        nc.tensor.matmul(b[:, 3 * P:T], hv[:, 2, hs], s_off[:, 3, :], start=False, stop=False)
                        ins = nc.tensor.matmul(b[:, 3 * P:T], hv[:, 3, hs], s_diag[:, 3, :],
                                               start=False, stop=True)
                    ins.then_inc(hg_mm, 1)

                def fox_scores_mm(h):
                    if h >= 1:
                        pe.wait_ge(fx_trout, 4 * h)
                    p0 = DHF * (h % 2)
                    rows = slice(p0, p0 + DHF)
                    for i in (3, 2, 1, 0):
                        o = fox_scores(i)
                        ext = (i + 1) * P
                        nc.tensor.matmul(o, ab[rows, 4 + h // 2, i * P:ext], fk[rows, h // 2, 0:ext],
                                         start=True, stop=False)
                        nc.tensor.matmul(o, head_row[0:HF, h, :], negc[:, 0:ext], start=False, stop=False)
                        ins = nc.tensor.matmul(o[:, i * P:ext], ident, cmask, start=False, stop=True)
                    ins.then_inc(fx_score, 1)

                def fox_transposes(h):
                    if h >= 1:
                        pe.wait_ge(fx_out, h)
                    pe.wait_ge(fx_norm, 4 * (h + 1))
                    for j in range(NT):
                        for i in range(j, NT):
                            ins = nc.tensor.transpose(fox_tr_bank(j)[:, (i - j) * P:(i - j + 1) * P],
                                                      probs[:, P_OFF[i] + j * P:P_OFF[i] + (j + 1) * P], ident)
                        ins.then_inc(fx_tr, 1)

                def fox_pv(h):
                    pe.wait_ge(fx_trout, 4 * (h + 1))
                    for j in range(NT):
                        ins = nc.tensor.matmul(bank[7][0:DHF, j * P:T], fv[:, j, h * DHF:(h + 1) * DHF],
                                               probs_t[:, PT_OFF[j]:PT_OFF[j] + PT_LEN[j]],
                                               start=j == 0, stop=j == NT - 1)
                    ins.then_inc(fx_pv, 1)

                for n in range(N_IN):
                    project(n)
                    for e in hgrn_slots(n):
                        hgrn_mm(e)
                    h = n - FX_STEP0
                    if 0 <= h <= 2 * HF:
                        if h == 0:
                            pe.wait_ge(c_ready, 1)
                        if h % 2 == 0 and h >= 2:
                            fox_pv(h // 2 - 1)
                        if h % 2 == 0 and h < 2 * HF:
                            fox_scores_mm(h // 2)
                        if h % 2 == 1:
                            fox_transposes(h // 2)
                    if n == 35:
                        for h in range(HH):
                            pe.wait_ge(on_sq, h + 1)
                            if h >= 2:
                                pe.wait_ge(on_mean, h - 1)
                            nc.tensor.matmul(bank[2 + h % 2][:, :], ones, kk[:, h, :], start=True, stop=True) \
                                .then_inc(on_mm, 1)

        ctx = ExitStack()
        with ctx:
            abs_ = sb(ctx, "ab_split", [P, 2, KD, T], F32R)
            gate = sb(ctx, "gate", [P, 2, 2, T])
            part = sb(ctx, "part", [P, 2, T])
            mbuf = sb(ctx, "mbuf", [P, 2, T])
            xbuf = sb(ctx, "xbuf", [P, 2, T])
            sqb = sb(ctx, "sqb", [P, 2, T])
            nb = sb(ctx, "nb", [P, 2, T])
            key_t = sb(ctx, "key_t", [P, NQ, NK])
            qt = sb(ctx, "qt", [P, 2, T])
            scs = sb(ctx, "scs", [P, 2, NT, NK])

            keys_in = sem("keys_in")
            ab_hi, ab_lo = sem("ab_hi"), sem("ab_lo")
            gate_in = [sem("gate_in0"), sem("gate_in1")]
            xres_in = [sem("xres_in0"), sem("xres_in1")]
            sg_ready, br_free, m_ready, m_hi, m_lo = (sem("sg_ready"), sem("br_free"), sem("m_ready"),
                                                      sem("m_hi"), sem("m_lo"))
            mchain = sem("mchain")
            h_ready, h_sq, h_ms, h_mean, h_root = sem("h_ready"), sem("h_sq"), sem("h_ms"), sem("h_mean"), \
                sem("h_root")
            x2_ready, x2_hi, x2_lo = sem("x2_ready"), sem("x2_hi"), sem("x2_lo")
            qt_ready, sc_mm, sc_out = sem("qt_ready"), sem("sc_mm"), sem("sc_out")
            sc_stored = [sem("sc_stored0"), sem("sc_stored1")]

            block = ctx.enter_context(nc.Block())

            def store_scores(sp, j):
                sp.wait_ge(sc_out, j + 1)
                sp.dma_start(scores_d[:, :, j, :].rearrange("i p k -> p i k"), scs[:, j % 2, :, :]) \
                    .then_inc(sc_stored[j % 2], 16)

            @block.sync
            def _(sp):
                def gates(c):
                    for b in range(2):
                        sp.dma_start(gate[:, c % 2, b, :], gates_d[KD * b + c, :, :]).then_inc(gate_in[c % 2], 16)

                def x_chunk(c):
                    sp.dma_start(xbuf[:, c % 2, :], xT[c * P:(c + 1) * P, :]).then_inc(xres_in[c % 2], 16)

                gates(0)
                gates(1)
                x_chunk(0)
                x_chunk(1)
                sp.dma_start(key_t[:, :, :], keys).then_inc(keys_in, 16)
                for n in range(BR0, U0):
                    load_unit(sp, n + LOAD_LEAD)
                    c = n - BR0
                    if 0 <= c < KD - 2:
                        sp.wait_ge(m_ready, c + 1)
                        gates(c + 2)
                    c = n - WO0
                    if 0 <= c < KD - 2:
                        sp.wait_ge(h_ready, c + 1)
                        x_chunk(c + 2)
                    j = n - WQ0 - 2
                    if j >= 0:
                        store_scores(sp, j)
                store_scores(sp, NQ - 2)
                store_scores(sp, NQ - 1)
                for s in range(2):
                    sp.wait_ge(sc_stored[s], 16 * (NQ // 2))

            @block.gpsimd
            def _(pool):
                for n in range(BR0, U0):
                    split_lo(pool, n + LEAD)

            @block.scalar
            def _(act_e):
                for k in range(KD):
                    act_e.activation(abs_[:, 0, k, :], ab[:, k, :], ACT.Copy).then_inc(ab_hi, 1)
                for n in range(BR0, U0):
                    split_hi(act_e, n + LEAD)
                    if n < WO0:
                        c = n - BR0
                        act_e.wait_ge(gate_in[c % 2], 32 * (c // 2 + 1))
                        act_e.activation(gate[:, c % 2, :, :], gate[:, c % 2, :, :], ACT.Sigmoid) \
                            .then_inc(sg_ready, 1)
                        act_e.wait_ge(m_ready, c + 1)
                        act_e.activation(act[:, 0, c, :], mbuf[:, c % 2, :], ACT.Copy).then_inc(m_hi, 1)
                    elif n < WQ0:
                        c = n - WO0
                        act_e.wait_ge(h_ready, c + 1)
                        if c >= 2:
                            act_e.wait_ge(h_ms, c - 1)
                        act_e.activation(sqb[:, c % 2, :], ab[:, c, :], ACT.Square).then_inc(h_sq, 1)
                        if c == KD - 1:
                            act_e.wait_ge(h_mean, 1)
                            act_e.activation(nb[:, 1, :], nb[:, 0, :], ACT.Sqrt).then_inc(h_root, 1)
                            for k in range(KD):
                                act_e.wait_ge(x2_ready, k + 1)
                                act_e.activation(act[:, 0, k, :], mbuf[:, k % 2, :], ACT.Copy) \
                                    .then_inc(x2_hi, 1)
                    else:
                        j = n - WQ0
                        act_e.wait_ge(unit_used, n + 1)
                        if j >= 2:
                            act_e.wait_ge(sc_mm, j - 1)
                        act_e.activation(qt[:, j % 2, :], bank[j % 2][:, :], ACT.Copy).then_inc(qt_ready, 1)

            @block.vector
            def _(dve):
                for k in range(KD):
                    dve.wait_ge(ab_hi, k + 1)
                    dve.tensor_tensor(abs_[:, 1, k, :], ab[:, k, :], abs_[:, 0, k, :].bitcast(F32),
                                      ALU.subtract).then_inc(ab_lo, 1)
                for c in range(KD):
                    dve.wait_ge(sg_ready, c + 1)
                    dve.wait_ge(unit_used, BR0 + c + 1)
                    for b in range(2):
                        ins = dve.tensor_tensor(part[:, b, :], bank[2 * (c % 2) + b][:, :], gate[:, c % 2, b, :],
                                                ALU.mult)
                    ins.then_inc(br_free, 1)
                    dve.wait_ge(br_free, c + 1)
                    dve.tensor_tensor(mbuf[:, c % 2, :], part[:, 0, :], part[:, 1, :], ALU.add) \
                        .then_inc(m_ready, 1)
                    dve.wait_ge(m_hi, c + 1)
                    dve.tensor_tensor(act[:, 1, c, :], mbuf[:, c % 2, :], act[:, 0, c, :].bitcast(F32),
                                      ALU.subtract).then_inc(m_lo, 1)
                for c in range(KD):
                    dve.wait_ge(xres_in[c % 2], 16 * (c // 2 + 1))
                    dve.wait_ge(unit_used, WO0 + c + 1)
                    dve.tensor_tensor(ab[:, c, :], bank[4 + c % 2][:, :], xbuf[:, c % 2, :], ALU.add) \
                        .then_inc(h_ready, 1)
                dve.wait_ge(h_ms, KD)
                dve.tensor_scalar(nb[:, 0, :], bank[6][:, :], 1.0 / D, EPS, ALU.mult, ALU.add).then_inc(h_mean, 1)
                dve.wait_ge(h_root, 1)
                dve.reciprocal(nb[:, 0, :], nb[:, 1, :]).then_inc(mchain, 1)
                dve.wait_ge(mchain, 1)

                def x2_rest(k):
                    dve.wait_ge(x2_hi, k + 1)
                    dve.tensor_tensor(act[:, 1, k, :], mbuf[:, k % 2, :], act[:, 0, k, :].bitcast(F32),
                                      ALU.subtract).then_inc(x2_lo, 1)

                for k in range(KD):
                    if k >= 2:
                        dve.wait_ge(x2_lo, k - 1)
                    dve.scalar_tensor_tensor(out=mbuf[:, k % 2, :], in0=ab[:, k, :], scalar=nrm[:, 1, k:k + 1],
                                             in1=nb[:, 0, :], op0=ALU.mult, op1=ALU.mult).then_inc(x2_ready, 1)
                    if k >= 1:
                        x2_rest(k - 1)
                x2_rest(KD - 1)
                for j in range(NQ):
                    dve.wait_ge(sc_mm, j + 1)
                    if j >= 2:
                        dve.wait_ge(sc_stored[j % 2], 16 * (j // 2))
                    dve.tensor_copy(scs[:, j % 2, :, :],
                                    bank[2 + j % 2][:, :].rearrange("p (i k) -> p i k", i=NT)) \
                        .then_inc(sc_out, 1)

            @block.tensor
            def _(pe):
                pe.wait_ge(ab_lo, KD)
                for c in range(KD):
                    n = BR0 + c
                    pe.wait_ge(lo_done, n + 1)
                    if c >= 2:
                        pe.wait_ge(br_free, c - 1)
                    for k in range(KD):
                        cs = slice(k * P, (k + 1) * P)
                        ins = passes(bank[2 * (c % 2) + k // 4][:, :], spl[:, 0, n % SPL, cs],
                                     spl[:, 1, n % SPL, cs], abs_[:, 0, k, :], abs_[:, 1, k, :],
                                     k % 4 == 0, k % 4 == 3)
                    ins.then_inc(unit_used, 1)

                def mean_square(c):
                    pe.wait_ge(h_sq, c + 1)
                    nc.tensor.matmul(bank[6][:, :], ones, sqb[:, c % 2, :], start=c == 0, stop=c == KD - 1) \
                        .then_inc(h_ms, 1)

                pe.wait_ge(m_lo, KD)
                for c in range(KD):
                    n = WO0 + c
                    pe.wait_ge(lo_done, n + 1)
                    if c >= 2:
                        pe.wait_ge(h_ready, c - 1)
                    unit_product(bank[4 + c % 2][:, :], n, act).then_inc(unit_used, 1)
                    if c >= 1:
                        mean_square(c - 1)
                mean_square(KD - 1)

                def key_scores(j):
                    if j == 0:
                        pe.wait_ge(keys_in, 16)
                    pe.wait_ge(qt_ready, j + 1)
                    if j >= 2:
                        pe.wait_ge(sc_out, j - 1)
                    for i in range(NT):
                        c = slice(i * P, (i + 1) * P)
                        ins = nc.tensor.matmul(bank[2 + j % 2][:, c], qt[:, j % 2, c], key_t[:, j, :],
                                               start=True, stop=True)
                    ins.then_inc(sc_mm, 1)

                for j in range(NQ):
                    n = WQ0 + j
                    pe.wait_ge(lo_done, n + 1)
                    if j == 0:
                        pe.wait_ge(x2_lo, KD)
                    if j >= 2:
                        pe.wait_ge(qt_ready, j - 1)
                    unit_product(bank[j % 2][:, :], n, act).then_inc(unit_used, 1)
                    if j >= 1:
                        key_scores(j - 1)
                key_scores(NQ - 1)

        ctx = ExitStack()
        with ctx:
            gl = sb(ctx, "gl", [P, 4, T])
            scb = sb(ctx, "scb", [P, PH, 2, NK])
            knock = sb(ctx, "knock", [P, 256])
            cand = sb(ctx, "cand", [P, TOPK, TOPK])
            top_v = sb(ctx, "top_v", [P, 2, TOPK])
            top_i = sb(ctx, "top_i", [P, 2, TOPK], U32)
            pair_v = sb(ctx, "pair_v", [P, PH, TOPK])
            pair_i = sb(ctx, "pair_i", [P, TOPK], U32)
            rank = sb(ctx, "rank", [P, 2, TOPK], U32)
            rank_f = sb(ctx, "rank_f", [P, 2, TOPK])
            key_f = sb(ctx, "key_f", [P, 2, TOPK])
            pick = sb(ctx, "pick", [P, 2, TOPK, TOPK])
            slot = sb(ctx, "slot", [P, 3, PH, TOPK])
            gsum = sb(ctx, "gsum", [P, 2, PH])
            slot_t = sb(ctx, "slot_t", [P, 5, T])
            blk = sb(ctx, "blk", [P, 5, 2 * TB])
            gbf = sb(ctx, "gbf", [P, P], BF16)
            gpart = sb(ctx, "gpart", [P, 2, P])
            iota_f = sb(ctx, "iota_f", [P, P])
            iota_b = sb(ctx, "iota_b", [P, P], BF16)
            hot = sb(ctx, "hot", [P, 2, QUAD, 4, NK], BF16)
            stage = sb(ctx, "stage", [P, 2, NC, TB])

            iota_in, sc_loaded = sem("iota_in"), sem("sc_loaded")
            heads_read = sem("heads_read")
            z_free = sem("z_free")
            gelu_stored = [sem(f"gelu_stored{i}") for i in range(4)]
            tk_shift, tk_exp, tk_slots, tk_tr = sem("tk_shift"), sem("tk_exp"), sem("tk_slots"), sem("tk_tr")
            tchain, bchain, iota_ready = sem("tchain"), sem("bchain"), sem("iota_ready")
            hot_ready = sem("hot_ready")
            quad_done = sem("quad_done")
            quad_out = sem("quad_out")
            stage_stored = [sem("stage_stored0"), sem("stage_stored1")]
            TILE_CHUNKS = 16
            QB = 2 * TB // QUAD
            BLOCK_CHUNKS = 8

            block = ctx.enter_context(nc.Block())

            @block.sync
            def _(sp):
                def load_u(n, group):
                    sp.wait_ge(lo_done, group + n - RAW + 1)
                    sp.dma_start(raw[:, n % RAW, :], u_t[group + (n - U0), :, :]).then_inc(unit_loaded[n % RAW], 16)

                sp.dma_start(iota_f[:, :], c_iota).then_inc(iota_in, 16)
                with sp.Fori(0, NC // 8 - 1) as g:
                    for j in range(8):
                        load_u(U0 + LOAD_LEAD + j, g * 8)
                for n in range(U0 + LOAD_LEAD + NC - 8, V0 + LOAD_LEAD):
                    load_unit(sp, n)

            @block.gpsimd
            def _(pool):
                with pool.Fori(0, NC // 8) as g:
                    for j in range(8):
                        split_lo(pool, U0 + LEAD + j, g * 8)

            @block.scalar
            def _(act_e):
                act_e.sem_inc(z_free, 2)
                act_e.sem_inc(quad_out, 4)
                for s in gelu_stored + stage_stored:
                    act_e.sem_inc(s, 16)

                def chunk(j, group):
                    n = U0 + j
                    split_hi(act_e, n + LEAD, group)
                    act_e.wait_ge(unit_used, group + n + 1)
                    act_e.wait_ge(gelu_stored[j % 4], group * 4 + 16 * (j // 4 + 1))
                    act_e.activation(gl[:, j % 4, :], bank[j % 2][:, :], ACT.Gelu).then_inc(z_free, 1)
                    act_e.wait_ge(z_free, group + j + 3)
                    act_e.dma_start(gelu_d[group + j, :, :], gl[:, j % 4, :]).then_inc(gelu_stored[j % 4], 16)

                with act_e.Fori(0, NT) as tile:
                    act_e.wait_ge(heads_read, tile + 1)
                    act_e.dma_start(scb[:, :, :, :].rearrange("p h s k -> p (h s) k"), scores_d[tile, :, :, :]) \
                        .then_inc(sc_loaded, 16)
                    for j in range(TILE_CHUNKS):
                        chunk(j, tile * TILE_CHUNKS)
                        if j == 13:
                            act_e.wait_ge(tk_shift, tile + 1)
                            act_e.activation(slot[:, 2, :, :], slot[:, 2, :, :], ACT.Exp).then_inc(tk_exp, 1)
                base = NT * TILE_CHUNKS
                with act_e.Fori(0, T // (2 * TB)) as b:
                    for j in range(BLOCK_CHUNKS):
                        chunk(base + j, b * BLOCK_CHUNKS)
                        for q in (2 * j, 2 * j + 1):
                            half, at = q // (QB // 2), q % (QB // 2) * QUAD
                            act_e.wait_ge(quad_done, b * QB + q + 3)
                            if at == 0:
                                act_e.wait_ge(stage_stored[half], b * 16 + 16)
                            act_e.activation(stage[:, half, :, at:at + QUAD],
                                             bank[4 + q % 4][:, :].rearrange("p (t c) -> p c t", t=QUAD),
                                             ACT.Copy).then_inc(quad_out, 1)
                        if j % 4 == 3:
                            half = j // 4
                            act_e.wait_ge(quad_out, b * QB + 4 + (half + 1) * (QB // 2))
                            act_e.dma_start(dense_d[b * 2 + half, :, :],
                                            stage[:, half, :, :].rearrange("p c t -> p (c t)")) \
                                .then_inc(stage_stored[half], 16)
                for s in range(4):
                    act_e.wait_ge(gelu_stored[s], 16 * (NC // 4 + 1))
                for s in range(2):
                    act_e.wait_ge(stage_stored[s], 16 * (T // (2 * TB) + 1))

            @block.vector
            def _(dve):
                dve.sem_inc(heads_read, 1)
                dve.wait_ge(iota_in, 16)
                dve.tensor_copy(iota_b[:, :], iota_f[:, :]).then_inc(iota_ready, 1)
                dve.wait_ge(iota_ready, 1)
                ranks = iota_f[:, 0:TOPK].unsqueeze(1).unsqueeze(1).to_broadcast([P, 2, TOPK, TOPK])

                with dve.Fori(0, NT) as tile:
                    count = [0]

                    def link(ins, hold=False):
                        count[0] += 1
                        ins.then_inc(tchain, 1)
                        dve.wait_ge(tchain, tile * TILE_LINKS + count[0])
                        if hold:
                            dve.nop(nofuse=True)

                    def top16(values, index, src, n):
                        rest = knock[:, 0:n]
                        link(dve.max(values[:, 0:8], src), hold=True)
                        dve.max_index(index[:, 0:8], values[:, 0:8], src)
                        link(dve.match_replace(rest, values[:, 0:8], src, LOWEST), hold=True)
                        link(dve.max(values[:, 8:16], rest), hold=True)
                        link(dve.max_index(index[:, 8:16], values[:, 8:16], rest), hold=True)

                    dve.wait_ge(sc_loaded, (tile + 1) * 16)
                    dve.nop(nofuse=True)
                    for h in range(PH):
                        for s in range(2):
                            top16(top_v[:, s, :], top_i[:, s, :], scb[:, h, s, :], NK)
                        dve.tensor_copy(key_f[:, :, :], top_i[:, :, :])
                        link(dve.tensor_tensor(cand[:, :, :], top_v[:, 0, :].unsqueeze(2).to_broadcast([P, TOPK, TOPK]),
                                               top_v[:, 1, :].unsqueeze(1).to_broadcast([P, TOPK, TOPK]), ALU.add),
                             hold=True)
                        top16(pair_v[:, h, :], pair_i[:, :], cand[:, :, :].rearrange("p a b -> p (a b)"),
                              TOPK * TOPK)
                        dve.tensor_scalar(rank[:, 0, :], pair_i[:, :], 4, None, ALU.logical_shift_right)
                        link(dve.tensor_scalar(rank[:, 1, :], pair_i[:, :], TOPK - 1, None, ALU.bitwise_and))
                        link(dve.tensor_copy(rank_f[:, :, :], rank[:, :, :]))
                        link(dve.tensor_tensor(pick[:, :, :, :],
                                               rank_f[:, :, :].unsqueeze(3).to_broadcast([P, 2, TOPK, TOPK]),
                                               ranks, ALU.is_equal))
                        link(dve.tensor_tensor(pick[:, :, :, :], pick[:, :, :, :],
                                               key_f[:, :, :].unsqueeze(2).to_broadcast([P, 2, TOPK, TOPK]),
                                               ALU.mult))
                        ins = dve.tensor_reduce(slot[:, 0:2, h, :], pick[:, :, :, :], AX.X, ALU.add)
                        if h < PH - 1:
                            link(ins, hold=True)
                    ins.then_inc(heads_read, 1)
                    dve.wait_ge(heads_read, tile + 2)
                    dve.tensor_tensor(slot[:, 2, :, :], pair_v[:, :, :],
                                      pair_v[:, :, 0:1].to_broadcast([P, PH, TOPK]), ALU.subtract) \
                        .then_inc(tk_shift, 1)
                    dve.wait_ge(tk_exp, tile + 1)
                    link(dve.tensor_reduce(gsum[:, 0, :], slot[:, 2, :, :], AX.X, ALU.add))
                    link(dve.reciprocal(gsum[:, 1, :], gsum[:, 0, :]))
                    dve.tensor_tensor(slot[:, 2, :, :], slot[:, 2, :, :],
                                      gsum[:, 1, :].unsqueeze(2).to_broadcast([P, PH, TOPK]), ALU.mult) \
                        .then_inc(tk_slots, 1)
                    dve.wait_ge(tk_tr, tile + 1)
                    tr = bank[2]
                    cols = bass.ds(tile * P, P)
                    dve.tensor_copy(slot_t[:, 0:2, cols], tr[:, 0:2 * P].rearrange("p (a t) -> p a t", a=2))
                    link(dve.tensor_copy(gpart[:, 0, :], tr[:, 2 * P:3 * P]))
                    for part_no in range(3):
                        link(dve.tensor_copy(gbf[:, :], gpart[:, 0, :]))
                        if part_no < 2:
                            link(dve.tensor_copy(gpart[:, 1, :], gbf[:, :]))
                            dve.tensor_copy(slot_t[:, 2 + part_no, cols], gbf[:, :])
                            link(dve.tensor_tensor(gpart[:, 0, :], gpart[:, 0, :], gpart[:, 1, :], ALU.subtract))
                        else:
                            link(dve.tensor_copy(slot_t[:, 4, cols], gbf[:, :]))
                    assert count[0] == TILE_LINKS, count[0]

                with dve.Fori(0, T // (2 * TB)) as b:
                    dve.tensor_copy(blk[:, :, :], slot_t[:, :, bass.ds(b * (2 * TB), 2 * TB)]).then_inc(bchain, 1)
                    dve.wait_ge(bchain, b + 1)
                    for q in range(QB):
                        dve.wait_ge(quad_done, b * QB + q + 1)
                        for t in range(QUAD):
                            col = q * QUAD + t
                            o = hot[:, q % 2, t, :, :]
                            dve.tensor_scalar(o[:, 0, :], iota_b[:, :], blk[:, 0, col:col + 1], None, ALU.is_equal)
                            for g in range(3):
                                ins = dve.tensor_scalar(o[:, 1 + g, :], iota_b[:, :], blk[:, 1, col:col + 1],
                                                        blk[:, 2 + g, col:col + 1], ALU.is_equal, ALU.mult)
                        ins.then_inc(hot_ready, 1)
                    dve.wait_ge(hot_ready, b * QB + QB)

            @block.tensor
            def _(pe):
                pe.sem_inc(quad_done, 2)

                def chunk(j, group):
                    n = U0 + j
                    pe.wait_ge(lo_done, group + n + 1)
                    pe.wait_ge(z_free, group + j + 1)
                    unit_product(bank[j % 2][:, :], n, act).then_inc(unit_used, 1)

                with pe.Fori(0, NT) as tile:
                    for j in range(TILE_CHUNKS):
                        chunk(j, tile * TILE_CHUNKS)
                    pe.wait_ge(tk_slots, tile + 1)
                    for a in range(3):
                        ins = nc.tensor.transpose(bank[2][:, a * P:(a + 1) * P],
                                                  slot[:, a, :, :].rearrange("p h k -> p (h k)"), ident)
                    ins.then_inc(tk_tr, 1)
                base = NT * TILE_CHUNKS
                with pe.Fori(0, T // (2 * TB)) as b:
                    for j in range(BLOCK_CHUNKS):
                        chunk(base + j, b * BLOCK_CHUNKS)
                        for q in (2 * j, 2 * j + 1):
                            pe.wait_ge(hot_ready, b * QB + q + 1)
                            pe.wait_ge(quad_out, b * QB + q + 1)
                            for t in range(QUAD):
                                o = hot[:, q % 2, t, :, :]
                                for g in range(3):
                                    ins = nc.tensor.matmul(bank[4 + q % 4][:, t * P:(t + 1) * P], o[:, 0, :],
                                                           o[:, 1 + g, :], start=g == 0, stop=g == 2)
                            ins.then_inc(quad_done, 1)

        ctx = ExitStack()
        with ctx:
            gate_in_sb = sb(ctx, "gate_in_sb", [P, 2, T // TB, 4, TB])
            gelu_in = sb(ctx, "gelu_in", [P, 2, 4, T])
            aw = sb(ctx, "aw", [P, 2, T])
            aws = sb(ctx, "aws", [P, 2, 4, T], F32R)
            fsq = sb(ctx, "fsq", [P, 2, T])
            fnb = sb(ctx, "fnb", [P, 2, T])

            mix_in = [sem("mix_in0"), sem("mix_in1")]
            a_mult, a_hi, a_lo = sem("a_mult"), sem("a_hi"), sem("a_lo")
            f_h, f_sq, f_ms, f_mean, f_root, f_inv, f_out, stored = (
                sem("f_h"), sem("f_sq"), sem("f_ms"), sem("f_mean"), sem("f_root"), sem("f_inv"),
                sem("f_out"), sem("stored"))
            BODY = 8
            BODIES = NC // BODY

            block = ctx.enter_context(nc.Block())

            @block.sync
            def _(sp):
                def mix(half, part_no):
                    sp.dma_start(gate_in_sb[:, half, :, :, :].rearrange("p b c t -> p b (c t)"),
                                 dense_d[:, :, bass.ds(part_no * (4 * TB), 4 * TB)].rearrange("b p x -> p b x")) \
                        .then_inc(mix_in[half], 16)
                    sp.dma_start(gelu_in[:, half, :, :],
                                 gelu_d[bass.ds(part_no * 4, 4), :, :].rearrange("c p t -> p c t")) \
                        .then_inc(mix_in[half], 16)

                def body(g, units):
                    for half in range(2):
                        for j in range(4):
                            n = V0 + LOAD_LEAD + 4 * half + j
                            if 4 * half + j < units:
                                sp.wait_ge(lo_done, g * BODY + n - RAW + 1)
                                sp.dma_start(raw[:, n % RAW, :], v_tab[:, g * BODY + (n - V0), :]) \
                                    .then_inc(unit_loaded[n % RAW], 16)
                        if units == BODY:
                            sp.wait_ge(a_mult, g * BODY + 4 * half + 4)
                            mix(half, g * 2 + half + 2)

                mix(0, 0)
                mix(1, 1)
                with sp.Fori(0, BODIES - 1) as g:
                    body(g, BODY)
                body(BODIES - 1, BODY - LOAD_LEAD)
                for c in range(KD):
                    sp.wait_ge(f_out, c + 1)
                    sp.dma_start(yT[c * P:(c + 1) * P, :], ab[:, c, :]).then_inc(stored, 16)
                sp.wait_ge(stored, 16 * KD)

            @block.gpsimd
            def _(pool):
                with pool.Fori(0, BODIES - 1) as g:
                    for j in range(BODY):
                        split_lo(pool, V0 + LEAD + j, g * BODY)
                for j in range(BODY - LEAD):
                    split_lo(pool, V0 + LEAD + j, (BODIES - 1) * BODY)

            @block.scalar
            def _(act_e):
                def body(g, units):
                    for j in range(BODY):
                        if j < units:
                            split_hi(act_e, V0 + LEAD + j, g * BODY)
                        act_e.wait_ge(a_mult, g * BODY + j + 1)
                        act_e.wait_ge(unit_used, g * BODY + (V0 + j - 3))
                        act_e.activation(aws[:, 0, j % 4, :], aw[:, j % 2, :], ACT.Copy).then_inc(a_hi, 1)

                with act_e.Fori(0, BODIES - 1) as g:
                    body(g, BODY)
                body(BODIES - 1, BODY - LEAD)
                for c in range(KD):
                    act_e.wait_ge(f_h, c + 1)
                    if c >= 2:
                        act_e.wait_ge(f_ms, c - 1)
                    act_e.activation(fsq[:, c % 2, :], ab[:, c, :], ACT.Square).then_inc(f_sq, 1)
                act_e.wait_ge(f_mean, 1)
                act_e.activation(fnb[:, 1, :], fnb[:, 0, :], ACT.Sqrt).then_inc(f_root, 1)

            @block.vector
            def _(dve):
                def body(g):
                    for j in range(BODY):
                        half = j // 4
                        if j % 4 == 0:
                            dve.wait_ge(mix_in[half], g * 32 + 32)
                        dve.tensor_tensor(aw[:, j % 2, :].rearrange("p (b t) -> p b t", t=TB),
                                          gelu_in[:, half, j % 4, :].rearrange("p (b t) -> p b t", t=TB),
                                          gate_in_sb[:, half, :, j % 4, :], ALU.mult).then_inc(a_mult, 1)
                        dve.wait_ge(a_hi, g * BODY + j + 1)
                        dve.tensor_tensor(aws[:, 1, j % 4, :], aw[:, j % 2, :],
                                          aws[:, 0, j % 4, :].bitcast(F32), ALU.subtract).then_inc(a_lo, 1)
                        dve.wait_ge(a_lo, g * BODY + j + 1)

                with dve.Fori(0, BODIES) as g:
                    body(g)
                dve.wait_ge(unit_used, N_UNITS)
                for c in range(KD):
                    dve.tensor_tensor(ab[:, c, :], bank[c][:, :], ab[:, c, :], ALU.add).then_inc(f_h, 1)
                dve.wait_ge(f_ms, KD)
                dve.tensor_scalar(fnb[:, 0, :], bank[0][:, :], 1.0 / D, EPS, ALU.mult, ALU.add).then_inc(f_mean, 1)
                dve.wait_ge(f_root, 1)
                dve.reciprocal(fnb[:, 0, :], fnb[:, 1, :]).then_inc(f_inv, 1)
                dve.wait_ge(f_inv, 1)
                for c in range(KD):
                    dve.scalar_tensor_tensor(out=ab[:, c, :], in0=ab[:, c, :], scalar=nrm[:, 2, c:c + 1],
                                             in1=fnb[:, 0, :], op0=ALU.mult, op1=ALU.mult).then_inc(f_out, 1)

            @block.tensor
            def _(pe):
                def body(g, first, last):
                    for j in range(BODY):
                        n = V0 + j
                        pe.wait_ge(lo_done, g * BODY + n + 1)
                        pe.wait_ge(a_lo, g * BODY + j + 1)
                        for d in range(KD):
                            c = slice(d * P, (d + 1) * P)
                            ins = passes(bank[d][:, :], spl[:, 0, n % SPL, c], spl[:, 1, n % SPL, c],
                                         aws[:, 0, j % 4, :], aws[:, 1, j % 4, :],
                                         first and j == 0, last and j == BODY - 1)
                        ins.then_inc(unit_used, 1)

                body(0, True, False)
                with pe.Fori(1, BODIES - 1) as g:
                    body(g, False, False)
                body(BODIES - 1, False, True)
                for c in range(KD):
                    pe.wait_ge(f_sq, c + 1)
                    nc.tensor.matmul(bank[0][:, :], ones, fsq[:, c % 2, :], start=c == 0, stop=c == KD - 1) \
                        .then_inc(f_ms, 1)


def kernel(x, norm_mix_w, w_in, hgrn_lb_logits, hgrn_norm_w, fox_f_bias, w_branch_hgrn, w_branch_fox,
           w_out, norm_ffn_w, peer_w_q, peer_sub_keys, peer_u, peer_v, norm_final_w):
    import numpy as np
    import concourse.bacc as bacc
    from concourse.bass_utils import run_bass_kernel_spmd

    c = np.ascontiguousarray
    f = [np.asarray(a) for a in (x, norm_mix_w, w_in, hgrn_lb_logits, hgrn_norm_w, fox_f_bias,
                                 w_branch_hgrn, w_branch_fox, w_out, norm_ffn_w, peer_w_q,
                                 peer_sub_keys, peer_u, peer_v, norm_final_w)]
    (x, norm_mix_w, w_in, hgrn_lb_logits, hgrn_norm_w, fox_f_bias, w_branch_hgrn, w_branch_fox,
     w_out, norm_ffn_w, peer_w_q, peer_sub_keys, peer_u, peer_v, norm_final_w) = f

    s, t = np.meshgrid(np.arange(P), np.arange(P), indexing="ij")
    c_f32 = np.stack([np.eye(P), np.where(t > s, LOWEST / 3, 0.0), np.ones((P, P))], axis=1)
    masks = []
    for l in range(LEVELS):
        hs = 64 >> l
        masks.append((s // (2 * hs) == t // (2 * hs)) & (s % (2 * hs) < hs) & (t % (2 * hs) >= hs))
    masks.append(s == t)

    arrays = {
        "xT": c(x[0].T),
        "w_in": c(w_in[0]),
        "norm_mix": c(norm_mix_w[0].reshape(KD, P).T),
        "lb_logits": c(hgrn_lb_logits.reshape(2, HH, P).transpose(2, 0, 1)),
        "hgrn_norm": c(hgrn_norm_w[0].reshape(HH, P).T),
        "fox_bias": c(fox_f_bias[0].reshape(HF, 1)),
        "w_a": c(w_branch_hgrn[0]),
        "w_b": c(w_branch_fox[0]),
        "w_out": c(w_out[0]),
        "norm_ffn": c(norm_ffn_w[0].reshape(KD, P).T),
        "w_q": c(peer_w_q[0]),
        "keys": c(peer_sub_keys[0].reshape(NQ, NK, P).transpose(2, 0, 1)),
        "u_t": c(peer_u[0].reshape(NK, NC, KD, P).transpose(1, 3, 2, 0).reshape(NC, P, W)),
        "v_tab": c(peer_v[0].reshape(NK, NC, D)),
        "norm_final": c(norm_final_w.reshape(KD, P).T),
        "c_f32": c_f32.astype(np.float32),
        "c_mask": c(np.stack(masks, axis=1).reshape(P, 8 * P).astype(np.float32)),
        "c_iota": c(np.broadcast_to(np.arange(P, dtype=np.float32), (P, P))),
    }
    nc = bacc.Bacc("TRN2", target_bir_lowering=False, num_devices=1)
    args = {n: nc.dram_tensor("in_" + n, a.shape, mybir.dt.from_np(a.dtype), kind="ExternalInput").ap()
            for n, a in arrays.items()}
    y = nc.dram_tensor("out_yT", (D, T), F32, kind="ExternalOutput").ap()
    build(nc, yT=y, **args)
    r = run_bass_kernel_spmd(nc, [{"in_" + n: a for n, a in arrays.items()}], core_ids=[0])
    return c(np.asarray(r.results[0]["out_yT"]).T)[None]
```

```python
import concourse.bass as bass
from concourse import mybir
from contextlib import ExitStack

F32 = mybir.dt.float32
F32R = mybir.dt.float32r
BF16 = mybir.dt.bfloat16
U32 = mybir.dt.uint32
ALU = mybir.AluOpType
ACT = mybir.ActivationFunctionType
AX = mybir.AxisListType

P = 128
D = 1024
T = 512
KD = D // P
NT = T // P
HH, HF = 4, 8
DHF = 64
PH = 8
NK = 128
NC = NK
TOPK = 16
EPS = 1e-6
W = KD * P
LOWEST = -3.0e38

RAW, SPL = 4, 8
LEAD = 4
LOAD_LEAD = 7

COL_HF = [512 + P * i for i in range(4)]
COL_HQ = [P * i for i in range(4)]
COL_HI = [1024 + P * i for i in range(4)]
COL_FV = [3072 + P * i for i in range(4)]
COL_FF = [3584]
COL_FQ = [2048 + P * i for i in range(4)]
COL_FK = [2560 + P * i for i in range(4)]
COL_GATES = [3592 + P * i for i in range(16)]
COL_HG = [1536 + P * i for i in range(4)]
COLS = COL_HF + COL_HQ + COL_HI + COL_FV + COL_FF + COL_FQ + COL_FK + COL_GATES + COL_HG
N_IN = len(COLS)
HF0, HQ0, HI0, FV0, FF0, FQ0, FK0, GA0, HG0 = 0, 4, 8, 12, 16, 17, 21, 25, 41
BR0 = N_IN
WO0 = BR0 + KD
WQ0 = WO0 + KD
NQ = PH * 2
U0 = WQ0 + NQ
V0 = U0 + NC
N_UNITS = V0 + NC

LEVELS = 7
EV_DIAG, EV_OFFX, EV_OFFY, EV_OUT, EV = 7, 8, 9, 10, 11
HG_STEP0 = 12
FX_STEP0 = 26
PT_OFF = [0, 512, 896, 1152]
PT_LEN = [512, 384, 256, 128]
P_OFF = [0, 128, 384, 768]
TB = 32
QUAD = 4
PARTS = 3

TILE_LINKS = 61


def exp_events(e):
    return (e // EV) * 8 + min(e % EV, 7) + (1 if e % EV > EV_OFFX else 0)


def hgrn_slots(n):
    lo = 2 * (n - HG_STEP0)
    return [e for e in (lo, lo + 1) if 0 <= e < EV * HH]


def exp_slot(e):
    return ((e // EV) * LEVELS + e % EV) % 3


def build(nc, xT, w_in, norm_mix, lb_logits, hgrn_norm, fox_bias, w_a, w_b, w_out, norm_ffn, w_q, keys,
          u_t, v_tab, norm_final, c_f32, c_mask, c_iota, yT):
    gates_d = nc.dram_tensor("gates_raw", (16, P, T), F32, kind="Internal").ap()
    scores_d = nc.dram_tensor("key_scores", (NT, P, NQ, NK), F32, kind="Internal").ap()
    gelu_d = nc.dram_tensor("gelu_ux", (NC, P, T), F32, kind="Internal").ap()
    dense_d = nc.dram_tensor("dense_gates", (T // TB, P, NC * TB), F32, kind="Internal").ap()

    outer = ExitStack()

    def sb(ctx, name, shape, dt=F32):
        return ctx.enter_context(nc.sbuf_tensor(name, shape, dt))

    def sem(name):
        return outer.enter_context(nc.semaphore(name))

    with outer:
        raw = sb(outer, "raw", [P, RAW, W])
        spl = sb(outer, "spl", [P, 2, SPL, W], F32R)
        act = sb(outer, "act", [P, 2, KD, T], F32R)
        ab = sb(outer, "ab", [P, KD, T])
        cst = sb(outer, "cst", [P, 3, P])
        nrm = sb(outer, "nrm", [P, 3, KD])
        ident, ones = cst[:, 0, :], cst[:, 2, :]
        bank = [outer.enter_context(nc.psum_tensor(f"bank{i}", [P, T], F32)) for i in range(8)]

        unit_loaded = [sem(f"unit_loaded{i}") for i in range(RAW)]
        hi_done, lo_done, unit_used = sem("hi_done"), sem("lo_done"), sem("unit_used")

        def unit_source(n):
            if n < BR0:
                return w_in[:, COLS[n]:COLS[n] + P].rearrange("(k p) c -> p k c", p=P)
            if n < WO0:
                return None
            if n < WQ0:
                c = (n - WO0) * P
                return w_out[:, c:c + P].rearrange("(k p) c -> p k c", p=P)
            if n < U0:
                c = (n - WQ0) * P
                return w_q[:, c:c + P].rearrange("(k p) c -> p k c", p=P)
            if n < V0:
                return u_t[n - U0, :, :]
            return v_tab[:, n - V0, :]

        def load_unit(sp, n):
            if n >= RAW:
                sp.wait_ge(lo_done, n - RAW + 1)
            s = n % RAW
            if BR0 <= n < WO0:
                c = (n - BR0) * P
                dst = raw[:, s, :].rearrange("p (k c) -> p k c", k=KD)
                sp.dma_start(dst[:, 0:4, :], w_a[:, c:c + P].rearrange("(k p) c -> p k c", p=P)) \
                    .then_inc(unit_loaded[s], 16)
                sp.dma_start(dst[:, 4:8, :], w_b[:, c:c + P].rearrange("(k p) c -> p k c", p=P)) \
                    .then_inc(unit_loaded[s], 16)
            elif n < U0:
                sp.dma_start(raw[:, s, :].rearrange("p (k c) -> p k c", k=KD), unit_source(n)) \
                    .then_inc(unit_loaded[s], 16)
            else:
                sp.dma_start(raw[:, s, :], unit_source(n)).then_inc(unit_loaded[s], 16)

        def loads_before(n, s):
            return sum(2 if BR0 <= m < WO0 else 1 for m in range(s, n + 1, RAW))

        def last_step(n):
            return n | 3 if HI0 <= n < FF0 else n

        def split_hi(eng, n, group=None):
            s = n % RAW
            extra = 0 if group is None else group * (16 // RAW)
            more = 0 if group is None else group
            eng.wait_ge(unit_loaded[s], extra + 16 * loads_before(n, s))
            if n >= SPL:
                eng.wait_ge(unit_used, more + last_step(n - SPL) + 1)
            eng.activation(spl[:, 0, n % SPL, :], raw[:, s, :], ACT.Copy).then_inc(hi_done, 1)

        def split_lo(eng, n, group=None):
            more = 0 if group is None else group
            eng.wait_ge(hi_done, more + n + 1)
            eng.tensor_tensor(spl[:, 1, n % SPL, :], raw[:, n % RAW, :],
                              spl[:, 0, n % SPL, :].bitcast(F32), ALU.subtract).then_inc(lo_done, 1)

        def passes(out, w_hi, w_lo, x_hi, x_lo, first, last):
            nc.tensor.matmul(out, w_hi, x_hi, start=first, stop=False)
            nc.tensor.matmul(out, w_hi, x_lo, start=False, stop=False)
            return nc.tensor.matmul(out, w_lo, x_hi, start=False, stop=last)

        def unit_product(out, n, src, chunks=None):
            for k in range(KD):
                if chunks:
                    chunks[0].wait_ge(chunks[1], k + 1)
                c = slice(k * P, (k + 1) * P)
                ins = passes(out, spl[:, 0, n % SPL, c], spl[:, 1, n % SPL, c],
                             src[:, 0, k, :], src[:, 1, k, :], k == 0, k == KD - 1)
            return ins

        ctx = ExitStack()
        with ctx:
            kc = sb(ctx, "kc", [P, 8, T])
            late = sb(ctx, "late", [P, KD, T])
            fk = sb(ctx, "fk", [P, 4, T])
            lev = sb(ctx, "lev", [P, 3, T])
            s_diag = sb(ctx, "s_diag", [P, NT, P])
            s_off = sb(ctx, "s_off", [P, 6, P])
            off_q = sb(ctx, "off_q", [P, 4, P])
            off_k = sb(ctx, "off_k", [P, 4, P])
            etot = sb(ctx, "etot", [P, 2])
            masks = sb(ctx, "masks", [P, 8, P], mybir.dt.uint8)
            head_row = sb(ctx, "head_row", [64 + HF, HF, P], BF16)
            negc3 = sb(ctx, "negc3", [64 + HF, T], BF16)
            masked = sb(ctx, "masked", [P, 2, P], BF16)
            negc = sb(ctx, "negc", [HF, T])
            negp = sb(ctx, "negp", [HF, T], BF16)
            probs = sb(ctx, "probs", [P, 1280])
            probs_t = sb(ctx, "probs_t", [P, 1280])
            stat = sb(ctx, "stat", [P, 4, 4])
            spill = sb(ctx, "spill", [P, 2, T])
            lbt = sb(ctx, "lbt", [P, 8, 4])
            hnw = sb(ctx, "hnw", [P, 4])
            fbias = sb(ctx, "fbias", [HF, 1])
            ones_row = sb(ctx, "ones_row", [P, P])
            ff = probs[0:HF, 0:2 * T].rearrange("p (a t) -> p a t", a=2)
            hv, fv = late[:, 0:4, :], late[:, 4:8, :]
            kk, cum = kc[:, 0:4, :], kc[:, 4:8, :]

            consts_in, mask_in, small_in = sem("consts_in"), sem("mask_in"), sem("small_in")
            x_in = [sem(f"x_in{q}") for q in range(4)]
            lb_diff, lb_exp = sem("lb_diff"), sem("lb_exp")
            squares, mean_mm, mean_ready, root_ready = [sem("squares0"), sem("squares1")], sem("mean_mm"), sem("mean_ready"), \
                sem("root_ready")
            xn_ready, xn_hi, xn_lo = sem("xn_ready"), sem("xn_hi"), sem("xn_lo")
            chain = sem("chain")
            achain = sem("achain")
            proj_out = [sem("proj_out0"), sem("proj_out1")]
            sig_ready, pool_zero, f_scan = sem("sig_ready"), sem("pool_zero"), sem("f_scan")
            f_ready, logf_ready = sem("f_ready"), sem("logf_ready")
            spilled = [sem("spilled0"), sem("spilled1")]
            ff_abs, ff_soft, c_ready = sem("ff_abs"), sem("ff_soft"), sem("c_ready")
            hg_diff, hg_exp, hg_pre, hg_mm, hg_post = sem("hg_diff"), sem("hg_exp"), sem("hg_pre"), \
                sem("hg_mm"), sem("hg_post")
            fx_score, fx_max, fx_exp, fx_norm, fx_tr, fx_trout, fx_pv, fx_out = (
                sem("fx_score"), sem("fx_max"), sem("fx_exp"), sem("fx_norm"), sem("fx_tr"),
                sem("fx_trout"), sem("fx_pv"), sem("fx_out"))
            on_sq, on_mm, on_mean, on_root = sem("on_sq"), sem("on_mm"), sem("on_mean"), sem("on_root")

            block = ctx.enter_context(nc.Block())

            def level_view(buf, h_size):
                return buf.rearrange("p (b u x) -> p b u x", u=2, x=h_size)

            @block.sync
            def _(sp):
                xv = xT.rearrange("(k p) t -> p k t", p=P)
                for q in range(4):
                    sp.dma_start(late[:, 2 * q:2 * q + 2, :], xv[:, 2 * q:2 * q + 2, :]).then_inc(x_in[q], 16)
                    if q == 0:
                        sp.dma_start(cst[:, :, :], c_f32).then_inc(consts_in, 16)
                sp.dma_start(nrm[:, 0, :], norm_mix).then_inc(small_in, 16)
                sp.dma_start(lbt[:, 0:2, :], lb_logits).then_inc(small_in, 16)
                sp.dma_start(nrm[:, 1, :], norm_ffn).then_inc(small_in, 16)
                sp.dma_start(nrm[:, 2, :], norm_final).then_inc(small_in, 16)
                sp.dma_start(hnw[:, :], hgrn_norm).then_inc(small_in, 16)
                sp.dma_start(fbias[:, :], fox_bias).then_inc(small_in, 16)
                sp.dma_start(probs[:, 0:8 * P], c_mask).then_inc(mask_in, 16)
                for n in range(LOAD_LEAD):
                    load_unit(sp, n)
                for n in range(N_IN):
                    load_unit(sp, n + LOAD_LEAD)
                    g = n - GA0 - 1
                    if 0 <= g < 16:
                        sp.wait_ge(proj_out[(n - 1) % 2], (n - 1) // 2 + 1)
                        sp.dma_start(gates_d[g, :, :], spill[:, g % 2, :]).then_inc(spilled[g % 2], 16)
                for s in range(2):
                    sp.wait_ge(spilled[s], 16 * 8)

            @block.gpsimd
            def _(pool):
                pool.memset(ones_row[:, :], 1.0).then_inc(pool_zero, 1)
                pool.memset(s_diag[:, :, :], 0.0).then_inc(pool_zero, 1)
                pool.memset(head_row[:, :, :], 0.0).then_inc(pool_zero, 1)
                pool.memset(negc3[:, :], 0.0).then_inc(pool_zero, 1)
                pool.wait_ge(consts_in, 16)
                pool.tensor_copy(masked[:, :, :], cst[:, 0:2, :]).then_inc(pool_zero, 1)
                pool.wait_ge(mask_in, 16)
                pool.tensor_copy(masks[:, :, :].rearrange("p l t -> p (l t)"), probs[:, 0:8 * P]) \
                    .then_inc(pool_zero, 1)
                for n in range(LEAD):
                    split_lo(pool, n)
                for n in range(N_IN):
                    split_lo(pool, n + LEAD)

            def act_fox_exp(act_e, h):
                for i in (3, 2, 1, 0):
                    act_e.wait_ge(fx_max, 4 * h + (4 - i if i > 1 else 4))
                    if h >= 1 and i == 3:
                        act_e.wait_ge(fx_tr, 4 * h)
                    act_e.activation(probs[:, P_OFF[i]:P_OFF[i] + (i + 1) * P], fox_scores(i), ACT.Exp,
                                     bias=stat[:, 0, i:i + 1],
                                     accum_out=stat[:, 1, i:i + 1]).then_inc(fx_exp, 1)

            def fox_scores(i):
                if i == 3:
                    return bank[4][:, :]
                if i == 2:
                    return bank[5][:, 0:384]
                return bank[6][:, 0:256] if i == 1 else bank[6][:, 256:384]

            def fox_tr_bank(j):
                return bank[[7, 4, 5, 6][j]][:, 0:PT_LEN[j]]

            def hgrn_exp(act_e, e):
                if e >= EV * HH:
                    return
                h, l = divmod(e, EV)
                if l < LEVELS:
                    b = exp_slot(e)
                    act_e.wait_ge(hg_diff, h * LEVELS + l + 1)
                    act_e.activation(lev[:, b, :], lev[:, b, :], ACT.Exp).then_inc(hg_exp, 1)
                elif l == EV_OFFX:
                    if h == 0:
                        act_e.wait_ge(f_scan, HH)
                    if h >= 1:
                        act_e.wait_ge(hg_mm, EV * (h - 1) + EV_OFFY + 1)
                    c = cum[:, h, :].rearrange("p (i x) -> p i x", i=NT)
                    act_e.activation(off_q[:, 0:2, :], c[:, 1:3, :], ACT.Exp)
                    act_e.activation(off_q[:, 3, :], c[:, 3, :], ACT.Exp)
                    for i, slot in ((0, 3), (1, 1), (2, 2)):
                        act_e.activation(off_k[:, slot, :], c[:, i, :], ACT.Exp,
                                         bias=c[:, i, P - 1:P], scale=-1.0)
                    act_e.activation(etot[:, 0:2], c[:, 1:3, P - 1], ACT.Exp).then_inc(hg_exp, 1)

            @block.scalar
            def _(act_e):
                act_e.wait_ge(pool_zero, 1)
                act_e.activation(stat[:, 0, :], ones_row[:, 0:4], ACT.Sqrt)
                for k in range(0, KD, 2):
                    act_e.wait_ge(x_in[k // 2], 16)
                    act_e.activation(kc[:, k, :], late[:, k, :], ACT.Square).then_inc(squares[0], 1)
                split_hi(act_e, 0)
                act_e.wait_ge(mean_ready, 1)
                act_e.activation(lev[:, 1, :], lev[:, 0, :], ACT.Sqrt).then_inc(root_ready, 1)
                for k in range(KD):
                    act_e.wait_ge(xn_ready, k + 1)
                    act_e.activation(act[:, 0, k, :], late[:, k, :], ACT.Copy).then_inc(xn_hi, 1)
                for n in range(1, LEAD):
                    split_hi(act_e, n)
                act_e.wait_ge(lb_diff, 1)
                act_e.activation(lbt[:, 2:4, :], lbt[:, 2:4, :], ACT.Exp).then_inc(lb_exp, 1)

                for n in range(N_IN):
                    split_hi(act_e, n + LEAD)
                    pr = bank[n % 2]
                    act_e.wait_ge(unit_used, n + 1)
                    if n < HQ0:
                        act_e.activation(kk[:, n, :], pr[:, :], ACT.Sigmoid).then_inc(proj_out[n % 2], 1)
                    elif n < HI0:
                        if n - HQ0 >= 2:
                            act_e.wait_ge(proj_out[n % 2], n // 2)
                        act_e.activation(lev[:, n % 2, :], pr[:, :], ACT.Sigmoid).then_inc(sig_ready, 1)
                    elif n < FV0:
                        act_e.activation(hv[:, n - HI0, :], pr[:, :], ACT.Copy).then_inc(proj_out[n % 2], 1)
                    elif n < FF0:
                        act_e.activation(fv[:, n - FV0, :], pr[:, :], ACT.Copy).then_inc(proj_out[n % 2], 1)
                    elif n == FF0:
                        pass
                    elif n < FK0:
                        act_e.activation(ab[:, 4 + n - FQ0, :], pr[:, :], ACT.Copy,
                                         scale=DHF ** -0.5).then_inc(proj_out[n % 2], 1)
                    elif n < GA0:
                        act_e.activation(fk[:, n - FK0, :], pr[:, :], ACT.Copy).then_inc(proj_out[n % 2], 1)
                    elif n < HG0:
                        g = n - GA0
                        if g >= 2:
                            act_e.wait_ge(spilled[g % 2], 16 * (g // 2))
                        act_e.activation(spill[:, g % 2, :], pr[:, :], ACT.Copy).then_inc(proj_out[n % 2], 1)
                    else:
                        if n - HG0 >= 2:
                            act_e.wait_ge(proj_out[n % 2], n // 2)
                        act_e.activation(lev[:, n % 2, :], pr[:, :], ACT.Sigmoid).then_inc(sig_ready, 1)
                    if n == FF0 + 1:
                        act_e.wait_ge(ff_abs, 1)
                        act_e.activation(ff[:, 1, :], ff[:, 1, :], ACT.Exp).then_inc(achain, 1)
                        act_e.wait_ge(achain, 1)
                        act_e.activation(ff[:, 1, :], ff[:, 1, :], ACT.Ln, bias=1.0).then_inc(ff_soft, 1)
                    if n == HI0 - 1:
                        for h in range(HH):
                            act_e.wait_ge(f_ready, h + 1)
                            act_e.activation(cum[:, h, :], cum[:, h, :], ACT.Ln).then_inc(logf_ready, 1)
                    if n == HG_STEP0 - 1:
                        hgrn_exp(act_e, 0)
                        hgrn_exp(act_e, 1)
                    for e in hgrn_slots(n):
                        hgrn_exp(act_e, e + 2)
                    h = n - FX_STEP0
                    if 0 <= h < 2 * HF:
                        if h % 2 == 0:
                            act_fox_exp(act_e, h // 2)
                        else:
                            for j in range(4):
                                act_e.wait_ge(fx_tr, 4 * (h // 2) + j + 1)
                                if h >= 2 and j == 0:
                                    act_e.wait_ge(fx_pv, h // 2)
                                act_e.activation(probs_t[:, PT_OFF[j]:PT_OFF[j] + PT_LEN[j]],
                                                 fox_tr_bank(j), ACT.Copy).then_inc(fx_trout, 1)
                    if n == 34:
                        for h in range(HH):
                            act_e.wait_ge(hg_post, EV * (h + 1))
                            act_e.activation(kk[:, h, :], ab[:, h, :], ACT.Square).then_inc(on_sq, 1)
                    if n == 36:
                        for h in range(HH):
                            act_e.wait_ge(on_mean, h + 1)
                            act_e.activation(cum[:, h, :], cum[:, h, :], ACT.Sqrt).then_inc(on_root, 1)

            @block.vector
            def _(dve):
                steps = [0]

                def link(ins):
                    steps[0] += 1
                    ins.then_inc(chain, 1)
                    dve.wait_ge(chain, steps[0])

                for k in range(1, KD, 2):
                    dve.wait_ge(x_in[k // 2], 16)
                    dve.tensor_tensor(kc[:, k, :], late[:, k, :], late[:, k, :], ALU.mult).then_inc(squares[1], 1)
                dve.wait_ge(small_in, 16 * 6)
                link(dve.tensor_tensor(lbt[:, 4, :], lbt[:, 0, :], lbt[:, 1, :], ALU.max))
                link(dve.tensor_tensor(lbt[:, 2, :], lbt[:, 0, :], lbt[:, 4, :], ALU.subtract))
                dve.tensor_tensor(lbt[:, 3, :], lbt[:, 1, :], lbt[:, 4, :], ALU.subtract).then_inc(lb_diff, 1)
                dve.wait_ge(mean_mm, 1)
                dve.tensor_scalar(lev[:, 0, :], bank[4][:, :], 1.0 / D, EPS, ALU.mult, ALU.add) \
                    .then_inc(mean_ready, 1)
                dve.wait_ge(root_ready, 1)
                link(dve.reciprocal(lev[:, 2, :], lev[:, 1, :]))
                for k in range(KD):
                    dve.scalar_tensor_tensor(out=late[:, k, :], in0=late[:, k, :], scalar=nrm[:, 0, k:k + 1],
                                             in1=lev[:, 2, :], op0=ALU.mult, op1=ALU.mult) \
                        .then_inc(xn_ready, 1)
                    if k >= 1:
                        dve.wait_ge(xn_hi, k)
                        dve.tensor_tensor(act[:, 1, k - 1, :], late[:, k - 1, :],
                                          act[:, 0, k - 1, :].bitcast(F32), ALU.subtract).then_inc(xn_lo, 1)
                dve.wait_ge(xn_hi, KD)
                dve.tensor_tensor(act[:, 1, KD - 1, :], late[:, KD - 1, :],
                                  act[:, 0, KD - 1, :].bitcast(F32), ALU.subtract).then_inc(xn_lo, 1)
                dve.wait_ge(lb_exp, 1)
                link(dve.tensor_tensor(lbt[:, 5, :], lbt[:, 2, :], lbt[:, 3, :], ALU.add))
                link(dve.reciprocal(lbt[:, 6, :], lbt[:, 5, :]))
                link(dve.tensor_tensor(lbt[:, 4, :], lbt[:, 2, :], lbt[:, 6, :], ALU.mult))
                link(dve.tensor_scalar(lbt[:, 5, :], lbt[:, 4, :], -1.0, 1.0, ALU.mult, ALU.add))
                link(dve.tensor_scalar(lbt[:, 6, :], lbt[:, 5, :], -1.0, None, ALU.mult))

                def pre1(e):
                    if e >= EV * HH or e % EV >= LEVELS:
                        return
                    h, l = divmod(e, EV)
                    hs = 64 >> l
                    c = level_view(cum[:, h, :], hs)
                    o = level_view(lev[:, exp_slot(e), :], hs)
                    mid = c[:, :, 0, hs - 1:hs].to_broadcast([P, T // (2 * hs), hs])
                    dve.tensor_tensor(o[:, :, 1, :], c[:, :, 1, :], mid, ALU.subtract)
                    dve.tensor_tensor(o[:, :, 0, :], mid, c[:, :, 0, :], ALU.subtract).then_inc(hg_diff, 1)

                def pre2(e):
                    if e >= EV * HH:
                        return
                    h, l = divmod(e, EV)
                    if l < LEVELS:
                        hs = 64 >> l
                        o = level_view(lev[:, exp_slot(e), :], hs)
                        q = level_view(ab[:, h, :], hs)
                        k = level_view(kk[:, h, :], hs)
                        dve.wait_ge(hg_exp, exp_events(e) + 1)
                        dve.tensor_tensor(o[:, :, 1, :], o[:, :, 1, :], q[:, :, 1, :], ALU.mult)
                        dve.tensor_tensor(o[:, :, 0, :], o[:, :, 0, :], k[:, :, 0, :], ALU.mult) \
                            .then_inc(hg_pre, 1)
                    elif l == EV_OFFX:
                        q = ab[:, h, :].rearrange("p (i x) -> p i x", i=NT)
                        k = kk[:, h, :].rearrange("p (i x) -> p i x", i=NT)
                        dve.wait_ge(hg_exp, exp_events(e) + 1)
                        dve.tensor_tensor(off_q[:, 0:2, :], off_q[:, 0:2, :], q[:, 1:3, :], ALU.mult)
                        dve.tensor_tensor(off_q[:, 3, :], off_q[:, 3, :], q[:, 3, :], ALU.mult)
                        dve.tensor_tensor(off_k[:, 1:3, :], off_k[:, 1:3, :], k[:, 1:3, :], ALU.mult)
                        link(dve.tensor_tensor(off_k[:, 3, :], off_k[:, 3, :], k[:, 0, :], ALU.mult))
                        dve.tensor_scalar(off_q[:, 2, :], off_q[:, 3, :], etot[:, 1:2], None, ALU.mult)
                        dve.tensor_scalar(off_k[:, 0, :], off_k[:, 3, :], etot[:, 0:1], None, ALU.mult) \
                            .then_inc(hg_pre, 1)

                def post(e):
                    h, l = divmod(e, EV)
                    b = bank[2 + e % 2]
                    dve.wait_ge(hg_mm, e + 1)
                    if l <= EV_DIAG:
                        if e >= 1:
                            dve.wait_ge(hg_post, e)
                        ins = dve.copy_predicated(s_diag[:, :, :],
                                                  masks[:, l:l + 1, :].to_broadcast([P, NT, P]),
                                                  b[:, :].rearrange("p (i x) -> p i x", i=NT))
                    elif l == EV_OFFX:
                        ins = dve.tensor_copy(s_off[:, 0:4, :], b[:, :].rearrange("p (i x) -> p i x", i=NT))
                    elif l == EV_OFFY:
                        ins = dve.tensor_copy(s_off[:, 4:6, :],
                                              b[:, 0:2 * P].rearrange("p (i x) -> p i x", i=2))
                    else:
                        ins = dve.tensor_copy(ab[:, h, :], b[:, :])
                    ins.then_inc(hg_post, 1)

                def fox_norm(h):
                    dve.wait_ge(fx_score, h + 1)
                    for i in (3, 2, 1, 0):
                        dve.tensor_reduce(stat[:, 0, i:i + 1], fox_scores(i), AX.X, ALU.max, negate=True) \
                            .then_inc(fx_max, 1)
                    for i in (3, 2, 1, 0):
                        dve.wait_ge(fx_exp, 4 * h + 4 - i)
                        link(dve.reciprocal(stat[:, 2, i:i + 1], stat[:, 1, i:i + 1]))
                        p = probs[:, P_OFF[i]:P_OFF[i] + (i + 1) * P]
                        dve.tensor_scalar(p, p, stat[:, 2, i:i + 1], None, ALU.mult).then_inc(fx_norm, 1)

                def fox_out(h):
                    p0 = DHF * (h % 2)
                    dve.wait_ge(fx_pv, h + 1)
                    dve.tensor_copy(ab[p0:p0 + DHF, 4 + h // 2, :], bank[7][0:DHF, :]).then_inc(fx_out, 1)

                for n in range(N_IN):
                    pr = bank[n % 2]
                    if n < HQ0:
                        dve.wait_ge(proj_out[n % 2], n // 2 + 1)
                        dve.tensor_scalar(cum[:, n, :], kk[:, n, :], lbt[:, 5, n:n + 1], lbt[:, 4, n:n + 1],
                                          ALU.mult, ALU.add).then_inc(f_ready, 1)
                        dve.tensor_scalar(kk[:, n, :], kk[:, n, :], lbt[:, 6, n:n + 1], lbt[:, 5, n:n + 1],
                                          ALU.mult, ALU.add)
                    elif n < HI0:
                        dve.wait_ge(sig_ready, n - HQ0 + 1)
                        dve.tensor_tensor(ab[:, n - HQ0, :], pr[:, :], lev[:, n % 2, :], ALU.mult) \
                            .then_inc(proj_out[n % 2], 1)
                    if n == HI0 - 1:
                        dve.wait_ge(pool_zero, 6)
                        for h in range(HH):
                            dve.wait_ge(logf_ready, h + 1)
                            for i in range(NT):
                                c = cum[:, h, i * P:(i + 1) * P]
                                ins = dve.tensor_tensor_scan(c, ones_row[:, :], c, 0.0, ALU.mult, ALU.add)
                            ins.then_inc(f_scan, 1)
                        dve.wait_ge(f_scan, HH)
                    if n == FF0:
                        dve.wait_ge(unit_used, n + 1)
                        dve.tensor_scalar(ff[:, 0, :], pr[0:HF, :], fbias[:, 0:1], None, ALU.add) \
                            .then_inc(proj_out[n % 2], 1)
                        dve.wait_ge(proj_out[n % 2], n // 2 + 1)
                        dve.scalar_tensor_tensor(out=ff[:, 1, :], in0=ff[:, 0, :], scalar=-1.0,
                                                 in1=ff[:, 0, :], op0=ALU.mult, op1=ALU.max)
                        link(dve.tensor_scalar(negc[:, :], ff[:, 0, :], 0.0, None, ALU.min))
                        dve.tensor_scalar(ff[:, 1, :], ff[:, 1, :], -1.0, None, ALU.mult).then_inc(ff_abs, 1)
                    if n == HI0 + 1:
                        for h in range(HF):
                            for r0 in (0, 32, 64):
                                ins = dve.tensor_copy(head_row[r0:r0 + HF, h, :],
                                                      ident[0:HF, h:h + 1].to_broadcast([HF, P]))
                        link(ins)
                    if n == FF0 + 2:
                        dve.wait_ge(ff_soft, 1)
                        link(dve.tensor_tensor(ff[:, 0, :], negc[:, :], ff[:, 1, :], ALU.subtract))
                        link(dve.memset(ff[:, 1, :], 1.0))
                        link(dve.tensor_tensor_scan(negc[:, :], ff[:, 1, :], ff[:, 0, :], 0.0,
                                                    ALU.mult, ALU.subtract))
                    if n == FF0 + 3:
                        for r0 in (0, 32, 64):
                            link(dve.tensor_copy(negp[:, :], negc[:, :]))
                            dve.tensor_copy(negc3[r0:r0 + HF, :], negp[:, :])
                            link(dve.tensor_tensor(negc[:, :], negc[:, :], negp[:, :], ALU.subtract))
                        dve.memset(ff[:, 1, :], 0.0).then_inc(c_ready, 1)
                    if n == HG_STEP0 - 1:
                        pre1(0)
                        pre1(1)
                        pre2(0)
                    for e in hgrn_slots(n):
                        pre2(e + 1)
                        pre1(e + 2)
                        post(e)
                    h = n - FX_STEP0
                    if 0 <= h <= 2 * HF and h % 2 == 0:
                        if h >= 2:
                            fox_out(h // 2 - 1)
                        if h < 2 * HF:
                            fox_norm(h // 2)
                    if n == 35:
                        for h in range(HH):
                            dve.wait_ge(on_mm, h + 1)
                            dve.tensor_scalar(cum[:, h, :], bank[2 + h % 2][:, :], 1.0 / P, EPS,
                                              ALU.mult, ALU.add).then_inc(on_mean, 1)
                    if 37 <= n < 41:
                        h = n - 37
                        dve.wait_ge(on_root, h + 1)
                        link(dve.reciprocal(cum[:, h, :], cum[:, h, :]))
                        link(dve.scalar_tensor_tensor(out=ab[:, h, :], in0=ab[:, h, :],
                                                      scalar=hnw[:, h:h + 1], in1=cum[:, h, :],
                                                      op0=ALU.mult, op1=ALU.mult))
                    if n >= HG0:
                        h = n - HG0
                        dve.wait_ge(sig_ready, 4 + h + 1)
                        link(dve.tensor_tensor(lev[:, n % 2, :], pr[:, :], lev[:, n % 2, :], ALU.mult))
                        dve.tensor_tensor(ab[:, h, :], ab[:, h, :], lev[:, n % 2, :], ALU.mult) \
                            .then_inc(proj_out[n % 2], 1)

            @block.tensor
            def _(pe):
                pe.wait_ge(consts_in, 16)
                for k in range(KD):
                    pe.wait_ge(squares[k % 2], k // 2 + 1)
                    ins = nc.tensor.matmul(bank[4][:, :], ones, kc[:, k, :], start=k == 0, stop=k == KD - 1)
                ins.then_inc(mean_mm, 1)

                def project(n):
                    pe.wait_ge(lo_done, last_step(n) + 1)
                    if n >= 2:
                        pe.wait_ge(proj_out[n % 2], n // 2)
                    out = bank[n % 2][:, :]
                    if HI0 <= n < FF0:
                        i, s0 = n % 4, (n & ~3) % SPL
                        t = slice(i * P, (i + 1) * P)
                        for k in range(KD):
                            c = slice(k * P, (k + 1) * P)
                            ins = passes(out, act[:, 0, k, t], act[:, 1, k, t], spl[:, 0, s0:s0 + 4, c],
                                         spl[:, 1, s0:s0 + 4, c], k == 0, k == KD - 1)
                    else:
                        ins = unit_product(out, n, act, (pe, xn_lo) if n == 0 else None)
                    ins.then_inc(unit_used, 1)

                def hgrn_mm(e):
                    h, l = divmod(e, EV)
                    b = bank[2 + e % 2]
                    if e >= 2:
                        pe.wait_ge(hg_post, e - 1)
                    hs = slice(h * P, (h + 1) * P)
                    if l < LEVELS:
                        pe.wait_ge(hg_pre, exp_events(e) + 1)
                        f = lev[:, exp_slot(e), :]
                        for i in range(NT):
                            c = slice(i * P, (i + 1) * P)
                            ins = nc.tensor.matmul(b[:, c], f[:, c], f[:, c], start=True, stop=True)
                    elif l == EV_DIAG:
                        for i in range(NT):
                            c = slice(i * P, (i + 1) * P)
                            ins = nc.tensor.matmul(b[:, c], kk[:, h, c], ab[:, h, c], start=True, stop=True)
                    elif l == EV_OFFX:
                        pe.wait_ge(hg_pre, exp_events(e) + 1)
                        for cols, s, q in ((slice(0, P), 3, slice(0, 1)), (slice(P, 3 * P), 0, slice(1, 3)),
                                           (slice(3 * P, T), 2, slice(3, 4))):
                            ins = nc.tensor.matmul(b[:, cols], off_k[:, s, :], off_q[:, q, :],
                                                   start=True, stop=True)
                    elif l == EV_OFFY:
                        ins = nc.tensor.matmul(b[:, 0:2 * P], off_k[:, 1, :], off_q[:, 1:3, :],
                                               start=True, stop=True)
                    else:
                        pe.wait_ge(hg_post, e)
                        nc.tensor.matmul(b[:, 0:P], hv[:, 0, hs], s_diag[:, 0, :], start=True, stop=False)
                        nc.tensor.matmul(b[:, P:T], hv[:, 0, hs], s_off[:, 0:3, :], start=False, stop=False)
                        nc.tensor.matmul(b[:, P:2 * P], hv[:, 1, hs], s_diag[:, 1, :], start=False, stop=False)
                        nc.tensor.matmul(b[:, 2 * P:T], hv[:, 1, hs], s_off[:, 4:6, :], start=False, stop=False)
                        nc.tensor.matmul(b[:, 2 * P:3 * P], hv[:, 2, hs], s_diag[:, 2, :],
                                         start=False, stop=False)
                        nc.tensor.matmul(b[:, 3 * P:T], hv[:, 2, hs], s_off[:, 3, :], start=False, stop=False)
                        ins = nc.tensor.matmul(b[:, 3 * P:T], hv[:, 3, hs], s_diag[:, 3, :],
                                               start=False, stop=True)
                    ins.then_inc(hg_mm, 1)

                def fox_scores_mm(h):
                    if h >= 1:
                        pe.wait_ge(fx_trout, 4 * h)
                    p0 = DHF * (h % 2)
                    rows = slice(p0, p0 + DHF)
                    for i in (3, 2, 1, 0):
                        o = fox_scores(i)
                        ext = (i + 1) * P
                        nc.tensor.matmul(o, ab[rows, 4 + h // 2, i * P:ext], fk[rows, h // 2, 0:ext],
                                         start=True, stop=False)
                        nc.tensor.matmul(o, head_row[:, h, :], negc3[:, 0:ext], start=False, stop=False)
                        ins = nc.tensor.matmul(o[:, i * P:ext], masked[:, 0, :], masked[:, 1, :],
                                               start=False, stop=True)
                    ins.then_inc(fx_score, 1)

                def fox_transposes(h):
                    if h >= 1:
                        pe.wait_ge(fx_out, h)
                    pe.wait_ge(fx_norm, 4 * (h + 1))
                    for j in range(NT):
                        for i in range(j, NT):
                            ins = nc.tensor.transpose(fox_tr_bank(j)[:, (i - j) * P:(i - j + 1) * P],
                                                      probs[:, P_OFF[i] + j * P:P_OFF[i] + (j + 1) * P], ident)
                        ins.then_inc(fx_tr, 1)

                def fox_pv(h):
                    pe.wait_ge(fx_trout, 4 * (h + 1))
                    for j in range(NT):
                        ins = nc.tensor.matmul(bank[7][0:DHF, j * P:T], fv[:, j, h * DHF:(h + 1) * DHF],
                                               probs_t[:, PT_OFF[j]:PT_OFF[j] + PT_LEN[j]],
                                               start=j == 0, stop=j == NT - 1)
                    ins.then_inc(fx_pv, 1)

                for n in range(N_IN):
                    project(n)
                    for e in hgrn_slots(n):
                        hgrn_mm(e)
                    h = n - FX_STEP0
                    if 0 <= h <= 2 * HF:
                        if h == 0:
                            pe.wait_ge(c_ready, 1)
                        if h % 2 == 0 and h >= 2:
                            fox_pv(h // 2 - 1)
                        if h % 2 == 0 and h < 2 * HF:
                            fox_scores_mm(h // 2)
                        if h % 2 == 1:
                            fox_transposes(h // 2)
                    if n == 35:
                        for h in range(HH):
                            pe.wait_ge(on_sq, h + 1)
                            if h >= 2:
                                pe.wait_ge(on_mean, h - 1)
                            nc.tensor.matmul(bank[2 + h % 2][:, :], ones, kk[:, h, :], start=True, stop=True) \
                                .then_inc(on_mm, 1)

        ctx = ExitStack()
        with ctx:
            scs = sb(ctx, "scs", [P, 2, NT, NK])
            abs_ = sb(ctx, "ab_split", [P, 2, KD, T], F32R)
            gate = sb(ctx, "gate", [P, 2, 2, T])
            part = sb(ctx, "part", [P, 2, T])
            mbuf = sb(ctx, "mbuf", [P, 2, T])
            xbuf = sb(ctx, "xbuf", [P, 2, T])
            sqb = sb(ctx, "sqb", [P, 2, T])
            nb = sb(ctx, "nb", [P, 2, T])
            key_t = sb(ctx, "key_t", [P, NQ, NK])
            qt = sb(ctx, "qt", [P, 2, T])

            keys_in = sem("keys_in")
            ab_hi, ab_lo = sem("ab_hi"), sem("ab_lo")
            gate_in = [sem("gate_in0"), sem("gate_in1")]
            xres_in = [sem("xres_in0"), sem("xres_in1")]
            sg_ready, br_free, m_ready, m_hi, m_lo = (sem("sg_ready"), sem("br_free"), sem("m_ready"),
                                                      sem("m_hi"), sem("m_lo"))
            mchain = sem("mchain")
            h_ready, h_sq, h_ms, h_mean, h_root = sem("h_ready"), sem("h_sq"), sem("h_ms"), sem("h_mean"), \
                sem("h_root")
            hw_ready, hw_hi, hw_lo = sem("hw_ready"), sem("hw_hi"), sem("hw_lo")
            x2_ready, x2_hi, x2_lo = sem("x2_ready"), sem("x2_hi"), sem("x2_lo")
            qt_ready, sc_mm, sc_out = sem("qt_ready"), sem("sc_mm"), sem("sc_out")
            sc_stored = [sem("sc_stored0"), sem("sc_stored1")]

            block = ctx.enter_context(nc.Block())

            def store_scores(sp, j):
                sp.wait_ge(sc_out, j + 1)
                sp.dma_start(scores_d[:, :, j, :].rearrange("i p k -> p i k"), scs[:, j % 2, :, :]) \
                    .then_inc(sc_stored[j % 2], 16)

            @block.sync
            def _(sp):
                def gates(c):
                    for b in range(2):
                        sp.dma_start(gate[:, c % 2, b, :], gates_d[KD * b + c, :, :]).then_inc(gate_in[c % 2], 16)

                def x_chunk(c):
                    sp.dma_start(xbuf[:, c % 2, :], xT[c * P:(c + 1) * P, :]).then_inc(xres_in[c % 2], 16)

                gates(0)
                gates(1)
                x_chunk(0)
                x_chunk(1)
                sp.dma_start(key_t[:, :, :], keys).then_inc(keys_in, 16)
                for n in range(BR0, U0):
                    load_unit(sp, n + LOAD_LEAD)
                    c = n - BR0
                    if 0 <= c < KD - 2:
                        sp.wait_ge(m_ready, c + 1)
                        gates(c + 2)
                    c = n - WO0
                    if 0 <= c < KD - 2:
                        sp.wait_ge(h_ready, c + 1)
                        x_chunk(c + 2)
                    j = n - WQ0 - 2
                    if j >= 0:
                        store_scores(sp, j)
                store_scores(sp, NQ - 2)
                store_scores(sp, NQ - 1)

            @block.gpsimd
            def _(pool):
                for n in range(BR0, U0):
                    split_lo(pool, n + LEAD)

            @block.scalar
            def _(act_e):
                for k in range(KD):
                    act_e.activation(abs_[:, 0, k, :], ab[:, k, :], ACT.Copy).then_inc(ab_hi, 1)
                for n in range(BR0, U0):
                    split_hi(act_e, n + LEAD)
                    if n < WO0:
                        c = n - BR0
                        act_e.wait_ge(gate_in[c % 2], 32 * (c // 2 + 1))
                        act_e.activation(gate[:, c % 2, :, :], gate[:, c % 2, :, :], ACT.Sigmoid) \
                            .then_inc(sg_ready, 1)
                        act_e.wait_ge(m_ready, c + 1)
                        act_e.activation(act[:, 0, c, :], mbuf[:, c % 2, :], ACT.Copy).then_inc(m_hi, 1)
                    elif n < WQ0:
                        c = n - WO0
                        act_e.wait_ge(h_ready, c + 1)
                        if c >= 2:
                            act_e.wait_ge(h_ms, c - 1)
                        act_e.activation(sqb[:, c % 2, :], ab[:, c, :], ACT.Square).then_inc(h_sq, 1)
                        act_e.wait_ge(hw_ready, c + 1)
                        act_e.activation(abs_[:, 0, c, :], mbuf[:, c % 2, :], ACT.Copy).then_inc(hw_hi, 1)
                    else:
                        k = n - WQ0
                        if k == 0:
                            act_e.wait_ge(h_mean, 1)
                            act_e.activation(nb[:, 1, :], nb[:, 0, :], ACT.Sqrt).then_inc(h_root, 1)
                        if k < KD:
                            act_e.wait_ge(x2_ready, k + 1)
                            act_e.activation(act[:, 0, k, :], mbuf[:, k % 2, :], ACT.Copy).then_inc(x2_hi, 1)

            @block.vector
            def _(dve):
                for k in range(KD):
                    dve.wait_ge(ab_hi, k + 1)
                    dve.tensor_tensor(abs_[:, 1, k, :], ab[:, k, :], abs_[:, 0, k, :].bitcast(F32),
                                      ALU.subtract).then_inc(ab_lo, 1)
                for c in range(KD):
                    dve.wait_ge(sg_ready, c + 1)
                    dve.wait_ge(unit_used, BR0 + c + 1)
                    for b in range(2):
                        ins = dve.tensor_tensor(part[:, b, :], bank[2 * (c % 2) + b][:, :], gate[:, c % 2, b, :],
                                                ALU.mult)
                    ins.then_inc(br_free, 1)
                    dve.wait_ge(br_free, c + 1)
                    dve.tensor_tensor(mbuf[:, c % 2, :], part[:, 0, :], part[:, 1, :], ALU.add) \
                        .then_inc(m_ready, 1)
                    dve.wait_ge(m_hi, c + 1)
                    dve.tensor_tensor(act[:, 1, c, :], mbuf[:, c % 2, :], act[:, 0, c, :].bitcast(F32),
                                      ALU.subtract).then_inc(m_lo, 1)
                for c in range(KD):
                    dve.wait_ge(xres_in[c % 2], 16 * (c // 2 + 1))
                    dve.wait_ge(unit_used, WO0 + c + 1)
                    dve.tensor_tensor(ab[:, c, :], bank[4 + c % 2][:, :], xbuf[:, c % 2, :], ALU.add) \
                        .then_inc(h_ready, 1)
                    dve.wait_ge(h_ready, c + 1)
                    if c >= 2:
                        dve.wait_ge(hw_lo, c - 1)
                    dve.tensor_scalar(mbuf[:, c % 2, :], ab[:, c, :], nrm[:, 1, c:c + 1], None, ALU.mult) \
                        .then_inc(hw_ready, 1)
                    dve.wait_ge(hw_hi, c + 1)
                    dve.tensor_tensor(abs_[:, 1, c, :], mbuf[:, c % 2, :], abs_[:, 0, c, :].bitcast(F32),
                                      ALU.subtract).then_inc(hw_lo, 1)
                dve.wait_ge(h_ms, KD)
                dve.tensor_scalar(nb[:, 0, :], bank[6][:, :], 1.0 / D, EPS, ALU.mult, ALU.add).then_inc(h_mean, 1)
                dve.wait_ge(h_root, 1)
                dve.reciprocal(nb[:, 0, :], nb[:, 1, :]).then_inc(mchain, 1)
                dve.wait_ge(mchain, 1)

                def scores_out(j):
                    dve.wait_ge(sc_mm, j + 1)
                    if j >= 2:
                        dve.wait_ge(sc_stored[j % 2], 16 * (j // 2))
                    dve.tensor_copy(scs[:, j % 2, :, :],
                                    bank[2 + j % 2][:, :].rearrange("p (i k) -> p i k", i=NT)) \
                        .then_inc(sc_out, 1)

                for j in range(NQ):
                    dve.wait_ge(unit_used, WQ0 + j + 1)
                    if j >= 2:
                        dve.wait_ge(sc_mm, j - 1)
                    dve.tensor_tensor(qt[:, j % 2, :], bank[j % 2][:, :], nb[:, 0, :], ALU.mult) \
                        .then_inc(qt_ready, 1)
                    if j < KD:
                        dve.wait_ge(x2_lo if j >= 2 else hw_lo, j - 1 if j >= 2 else KD)
                        dve.scalar_tensor_tensor(out=mbuf[:, j % 2, :], in0=ab[:, j, :],
                                                 scalar=nrm[:, 1, j:j + 1], in1=nb[:, 0, :],
                                                 op0=ALU.mult, op1=ALU.mult).then_inc(x2_ready, 1)
                        dve.wait_ge(x2_hi, j + 1)
                        dve.tensor_tensor(act[:, 1, j, :], mbuf[:, j % 2, :], act[:, 0, j, :].bitcast(F32),
                                          ALU.subtract).then_inc(x2_lo, 1)
                    if j >= 1:
                        scores_out(j - 1)
                scores_out(NQ - 1)

            @block.tensor
            def _(pe):
                for c in range(KD):
                    n = BR0 + c
                    pe.wait_ge(lo_done, n + 1)
                    if c >= 2:
                        pe.wait_ge(br_free, c - 1)
                    for k in range(KD):
                        cs = slice(k * P, (k + 1) * P)
                        if c == 0:
                            pe.wait_ge(ab_lo, k + 1)
                        ins = passes(bank[2 * (c % 2) + k // 4][:, :], spl[:, 0, n % SPL, cs],
                                     spl[:, 1, n % SPL, cs], abs_[:, 0, k, :], abs_[:, 1, k, :],
                                     k % 4 == 0, k % 4 == 3)
                    ins.then_inc(unit_used, 1)

                def mean_square(c):
                    pe.wait_ge(h_sq, c + 1)
                    nc.tensor.matmul(bank[6][:, :], ones, sqb[:, c % 2, :], start=c == 0, stop=c == KD - 1) \
                        .then_inc(h_ms, 1)

                for c in range(KD):
                    n = WO0 + c
                    pe.wait_ge(lo_done, n + 1)
                    if c >= 2:
                        pe.wait_ge(h_ready, c - 1)
                    unit_product(bank[4 + c % 2][:, :], n, act, (pe, m_lo) if c == 0 else None) \
                        .then_inc(unit_used, 1)
                    if c >= 2:
                        mean_square(c - 2)

                def key_scores(j):
                    if j == 0:
                        pe.wait_ge(keys_in, 16)
                    pe.wait_ge(qt_ready, j + 1)
                    if j >= 2:
                        pe.wait_ge(sc_out, j - 1)
                    for i in range(NT):
                        c = slice(i * P, (i + 1) * P)
                        ins = nc.tensor.matmul(bank[2 + j % 2][:, c], qt[:, j % 2, c], key_t[:, j, :],
                                               start=True, stop=True)
                    ins.then_inc(sc_mm, 1)

                for j in range(NQ):
                    n = WQ0 + j
                    pe.wait_ge(lo_done, n + 1)
                    if j >= 2:
                        pe.wait_ge(qt_ready, j - 1)
                    unit_product(bank[j % 2][:, :], n, abs_, (pe, hw_lo) if j == 0 else None).then_inc(unit_used, 1)
                    if j == 0:
                        mean_square(KD - 2)
                        mean_square(KD - 1)
                    if j >= 1:
                        key_scores(j - 1)
                key_scores(NQ - 1)

        mixbuf = sb(outer, "mixbuf", [P, 2 * NC * TB])
        stage = mixbuf[:, :].rearrange("p (s c t) -> p s c t", s=2, c=NC)
        gates_in = mixbuf[:, 0:8 * T].rearrange("p (s b c t) -> p s b c t", s=2, c=4, t=TB)
        gelu_in = mixbuf[:, 8 * T:16 * T].rearrange("p (s c t) -> p s c t", s=2, c=4)
        mix_in = [sem("mix_in0"), sem("mix_in1")]

        def mix(sp, half, part_no):
            sp.dma_start(gates_in[:, half, :, :, :].rearrange("p b c t -> p b (c t)"),
                         dense_d[:, :, bass.ds(part_no * (4 * TB), 4 * TB)].rearrange("b p x -> p b x")) \
                .then_inc(mix_in[half], 16)
            sp.dma_start(gelu_in[:, half, :, :],
                         gelu_d[bass.ds(part_no * 4, 4), :, :].rearrange("c p t -> p c t")) \
                .then_inc(mix_in[half], 16)

        ctx = ExitStack()
        with ctx:
            gl = sb(ctx, "gl", [P, 4, T])
            knock = sb(ctx, "knock", [P, 4 * NK])
            cand = sb(ctx, "cand", [P, 2, TOPK, TOPK])
            top_v = sb(ctx, "top_v", [P, 2, 2, TOPK])
            top_i = sb(ctx, "top_i", [P, 2, 2, TOPK], U32)
            pair_v = sb(ctx, "pair_v", [P, PH, TOPK])
            pair_i = sb(ctx, "pair_i", [P, 2, TOPK], U32)
            rank = sb(ctx, "rank", [P, 2, 2, TOPK], U32)
            rank_f = sb(ctx, "rank_f", [P, 2, 2, TOPK])
            key_f = sb(ctx, "key_f", [P, 2, 2, TOPK])
            pick = sb(ctx, "pick", [P, 4, TOPK, TOPK])
            slot = sb(ctx, "slot", [P, 3, PH, TOPK])
            gsum = sb(ctx, "gsum", [P, 2, PH])
            slot_t = sb(ctx, "slot_t", [P, 2 + PARTS, T], BF16)
            blk = sb(ctx, "blk", [P, 2 + PARTS, 2 * TB], BF16)
            remain = sb(ctx, "remain", [P, P])
            iota_f = sb(ctx, "iota_f", [P, P])
            iota_q = sb(ctx, "iota_q", [P, NK, QUAD], BF16)
            scb = sb(ctx, "scb", [P, 2, PH, 2, NK])
            hots = scb[:, :, :, :, :].rearrange("p b h s k -> p (b h s k)").bitcast(BF16)
            size = NK * QUAD
            hot = hots[:, 0:4 * size].rearrange("p (b s k t) -> p b s k t", b=2, s=2, t=QUAD)
            hotg = hots[:, 4 * size:(4 + 2 * PARTS) * size] \
                .rearrange("p (b g k t) -> p b g k t", b=2, g=PARTS, t=QUAD)

            iota_in = sem("iota_in")
            sc_loaded = [sem("sc_loaded0"), sem("sc_loaded1")]
            heads_read = sem("heads_read")
            z_free = sem("z_free")
            gelu_stored = [sem(f"gelu_stored{i}") for i in range(4)]
            tk_shift, tk_exp, tk_slots, tk_tr = sem("tk_shift"), sem("tk_exp"), sem("tk_slots"), sem("tk_tr")
            tchain, bchain = sem("tchain"), sem("bchain")
            hot_ready, hotg_ready = sem("hot_ready"), sem("hotg_ready")
            quad_done = sem("quad_done")
            quad_out = sem("quad_out")
            stage_stored = [sem("stage_stored0"), sem("stage_stored1")]
            HEAD_CHUNKS = 2
            TILE_CHUNKS = 12
            PAIR_CHUNKS = 2 * TILE_CHUNKS
            GATE_BODIES = T // (2 * TB)
            QB = 2 * TB // QUAD
            BLOCK_CHUNKS = 8

            block = ctx.enter_context(nc.Block())

            @block.sync
            def _(sp):
                def load_u(n, group):
                    sp.wait_ge(lo_done, group + n - RAW + 1)
                    sp.dma_start(raw[:, n % RAW, :], u_t[group + (n - U0), :, :]).then_inc(unit_loaded[n % RAW], 16)

                for s in range(2):
                    sp.wait_ge(sc_stored[s], 16 * (NQ // 2))
                sp.dma_start(scb[:, 0, :, :, :].rearrange("p h s k -> p (h s) k"), scores_d[0, :, :, :]) \
                    .then_inc(sc_loaded[0], 16)
                sp.dma_start(iota_f[:, :], c_iota).then_inc(iota_in, 16)
                early = (2 * PAIR_CHUNKS + GATE_BODIES * BLOCK_CHUNKS) // 8
                with sp.Fori(0, early) as g:
                    for j in range(8):
                        load_u(U0 + LOAD_LEAD + j, g * 8)
                rest = U0 + LOAD_LEAD + 8 * early
                for n in range(rest, rest + 5):
                    load_unit(sp, n)
                for half in range(2):
                    sp.wait_ge(stage_stored[half], 16 * (GATE_BODIES + 1))
                for slot_no in range(4):
                    sp.wait_ge(gelu_stored[slot_no], 16 * 3)
                mix(sp, 0, 0)
                mix(sp, 1, 1)
                for n in range(rest + 5, V0 + LOAD_LEAD):
                    load_unit(sp, n)

            @block.gpsimd
            def _(pool):
                with pool.Fori(0, NC // 8) as g:
                    for j in range(8):
                        split_lo(pool, U0 + LEAD + j, g * 8)

            @block.scalar
            def _(act_e):
                act_e.sem_inc(z_free, 2)
                act_e.sem_inc(quad_out, 4)
                for s in gelu_stored + stage_stored:
                    act_e.sem_inc(s, 16)

                def chunk(j, group):
                    n = U0 + j
                    split_hi(act_e, n + LEAD, group)
                    act_e.wait_ge(unit_used, group + n + 1)
                    act_e.wait_ge(gelu_stored[j % 4], group * 4 + 16 * (j // 4 + 1))
                    act_e.activation(gl[:, j % 4, :], bank[j % 2][:, :], ACT.Gelu).then_inc(z_free, 1)
                    act_e.wait_ge(z_free, group + j + 3)
                    act_e.dma_start(gelu_d[group + j, :, :], gl[:, j % 4, :]).then_inc(gelu_stored[j % 4], 16)

                for j in range(HEAD_CHUNKS):
                    chunk(j, 0)
                with act_e.Fori(0, NT // 2) as pair:
                    for s in range(2):
                        tile = pair * 2 + s
                        for j in range(TILE_CHUNKS):
                            chunk(HEAD_CHUNKS + s * TILE_CHUNKS + j, pair * PAIR_CHUNKS)
                            if j == TILE_CHUNKS // 3:
                                act_e.wait_ge(heads_read, tile + 1)
                                following = tile + 1 if s == 0 else pair * -2 + 2
                                act_e.dma_start(scb[:, 1 - s, :, :, :].rearrange("p h s k -> p (h s) k"),
                                                scores_d[following, :, :, :]).then_inc(sc_loaded[1 - s], 16)
                            if j == TILE_CHUNKS - 2:
                                act_e.wait_ge(tk_shift, tile + 1)
                                act_e.activation(slot[:, 2, :, :], slot[:, 2, :, :], ACT.Exp).then_inc(tk_exp, 1)
                base = HEAD_CHUNKS + 2 * PAIR_CHUNKS
                with act_e.Fori(0, GATE_BODIES) as b:
                    for j in range(BLOCK_CHUNKS):
                        chunk(base + j, b * BLOCK_CHUNKS)
                        for q in (2 * j, 2 * j + 1):
                            half, at = q // (QB // 2), q % (QB // 2) * QUAD
                            act_e.wait_ge(quad_done, b * QB + q + 3)
                            if at == 0:
                                act_e.wait_ge(stage_stored[half], b * 16 + 16)
                            act_e.activation(stage[:, half, :, at:at + QUAD],
                                             bank[4 + q % 4][:, :].rearrange("p (t c) -> p c t", t=QUAD),
                                             ACT.Copy).then_inc(quad_out, 1)
                        if j % 4 == 3:
                            half = j // 4
                            act_e.wait_ge(quad_out, b * QB + 4 + (half + 1) * (QB // 2))
                            act_e.dma_start(dense_d[b * 2 + half, :, :],
                                            stage[:, half, :, :].rearrange("p c t -> p (c t)")) \
                                .then_inc(stage_stored[half], 16)
                base += GATE_BODIES * BLOCK_CHUNKS
                for j in range(NC - base):
                    chunk(base + j, 0)
            @block.vector
            def _(dve):
                dve.sem_inc(heads_read, 1)
                dve.wait_ge(iota_in, 16)
                ranks = iota_f[:, 0:TOPK].unsqueeze(1).unsqueeze(1).to_broadcast([P, 4, TOPK, TOPK])

                dve.tensor_copy(iota_q[:, :, :], iota_f[:, :].unsqueeze(2).to_broadcast([P, NK, QUAD])) \
                    .then_inc(iota_in, 1)

                def retrieve_tile(pair, s):
                    tile = pair * 2 + s
                    count = [0]

                    def link(ins, hold=False):
                        count[0] += 1
                        ins.then_inc(tchain, 1)
                        dve.wait_ge(tchain, tile * TILE_LINKS + count[0])
                        if hold:
                            dve.nop(nofuse=True)

                    def top16(lists, n):
                        rest = [knock[:, m * n:(m + 1) * n] for m in range(len(lists))]
                        for values, index, src in lists:
                            ins = dve.max(values[:, 0:8], src)
                        link(ins, hold=True)
                        for values, index, src in lists:
                            dve.max_index(index[:, 0:8], values[:, 0:8], src)
                        for (values, index, src), left in zip(lists, rest):
                            ins = dve.match_replace(left, values[:, 0:8], src, LOWEST)
                        link(ins, hold=True)
                        for (values, index, src), left in zip(lists, rest):
                            ins = dve.max(values[:, 8:16], left)
                        link(ins, hold=True)
                        for (values, index, src), left in zip(lists, rest):
                            ins = dve.max_index(index[:, 8:16], values[:, 8:16], left)
                        link(ins, hold=True)

                    dve.wait_ge(sc_loaded[s], pair * 16 + 16)
                    dve.nop(nofuse=True)
                    for h in range(0, PH, 2):
                        top16([(top_v[:, a, side, :], top_i[:, a, side, :],
                                scb[:, s, h + a, side, :]) for a in range(2) for side in range(2)], NK)
                        dve.tensor_copy(key_f[:, :, :, :], top_i[:, :, :, :])
                        link(dve.tensor_tensor(cand[:, :, :, :],
                                               top_v[:, :, 0, :].unsqueeze(3).to_broadcast([P, 2, TOPK, TOPK]),
                                               top_v[:, :, 1, :].unsqueeze(2).to_broadcast([P, 2, TOPK, TOPK]),
                                               ALU.add), hold=True)
                        top16([(pair_v[:, h + a, :], pair_i[:, a, :],
                                cand[:, a, :, :].rearrange("p a b -> p (a b)")) for a in range(2)], TOPK * TOPK)
                        dve.tensor_scalar(rank[:, :, 0, :], pair_i[:, :, :], 4, None, ALU.logical_shift_right)
                        link(dve.tensor_scalar(rank[:, :, 1, :], pair_i[:, :, :], TOPK - 1, None, ALU.bitwise_and))
                        link(dve.tensor_copy(rank_f[:, :, :, :], rank[:, :, :, :]))
                        link(dve.tensor_tensor(pick[:, :, :, :],
                                               rank_f[:, :, :, :].rearrange("p a s k -> p (a s) k")
                                               .unsqueeze(3).to_broadcast([P, 4, TOPK, TOPK]),
                                               ranks, ALU.is_equal))
                        link(dve.tensor_tensor(pick[:, :, :, :], pick[:, :, :, :],
                                               key_f[:, :, :, :].rearrange("p a s k -> p (a s) k")
                                               .unsqueeze(2).to_broadcast([P, 4, TOPK, TOPK]), ALU.mult))
                        for a in range(2):
                            ins = dve.tensor_reduce(slot[:, 0:2, h + a, :], pick[:, 2 * a:2 * a + 2, :, :],
                                                    AX.X, ALU.add)
                        if h < PH - 2:
                            link(ins, hold=True)
                    ins.then_inc(heads_read, 1)
                    dve.wait_ge(heads_read, tile + 2)
                    dve.tensor_tensor(slot[:, 2, :, :], pair_v[:, :, :],
                                      pair_v[:, :, 0:1].to_broadcast([P, PH, TOPK]), ALU.subtract) \
                        .then_inc(tk_shift, 1)
                    dve.wait_ge(tk_exp, tile + 1)
                    link(dve.tensor_reduce(gsum[:, 0, :], slot[:, 2, :, :], AX.X, ALU.add))
                    link(dve.reciprocal(gsum[:, 1, :], gsum[:, 0, :]))
                    dve.tensor_tensor(slot[:, 2, :, :], slot[:, 2, :, :],
                                      gsum[:, 1, :].unsqueeze(2).to_broadcast([P, PH, TOPK]), ALU.mult) \
                        .then_inc(tk_slots, 1)
                    dve.wait_ge(tk_tr, tile + 1)
                    tr = bank[2]
                    cols = bass.ds(tile * P, P)
                    dve.tensor_copy(slot_t[:, 0:2, cols], tr[:, 0:2 * P].rearrange("p (a t) -> p a t", a=2))
                    link(dve.tensor_copy(slot_t[:, 2, cols], tr[:, 2 * P:3 * P]))
                    link(dve.tensor_tensor(remain[:, :], tr[:, 2 * P:3 * P], slot_t[:, 2, cols], ALU.subtract))
                    link(dve.tensor_copy(slot_t[:, 3, cols], remain[:, :]))
                    link(dve.tensor_tensor(slot_t[:, 4, cols], remain[:, :], slot_t[:, 3, cols], ALU.subtract))
                    assert count[0] == TILE_LINKS, count[0]

                with dve.Fori(0, NT // 2) as pair:
                    for s in range(2):
                        retrieve_tile(pair, s)

                dve.wait_ge(iota_in, 17)
                dve.wait_ge(sc_loaded[0], 16 * (NT // 2 + 1))
                with dve.Fori(0, GATE_BODIES) as b:
                    dve.tensor_copy(blk[:, :, :], slot_t[:, :, bass.ds(b * (2 * TB), 2 * TB)]) \
                        .then_inc(bchain, 1)
                    dve.wait_ge(bchain, b + 1)
                    for q in range(QB):
                        dve.wait_ge(quad_done, b * QB + q + 1)
                        cols = slice(q * QUAD, (q + 1) * QUAD)
                        dve.tensor_tensor(hot[:, q % 2, :, :, :],
                                          iota_q[:, :, :].unsqueeze(1).to_broadcast([P, 2, NK, QUAD]),
                                          blk[:, 0:2, cols].unsqueeze(2).to_broadcast([P, 2, NK, QUAD]),
                                          ALU.is_equal).then_inc(hot_ready, 1)
                        dve.wait_ge(hot_ready, b * QB + q + 1)
                        dve.tensor_tensor(hotg[:, q % 2, :, :, :],
                                          hot[:, q % 2, 1, :, :].unsqueeze(1).to_broadcast([P, PARTS, NK, QUAD]),
                                          blk[:, 2:2 + PARTS, cols].unsqueeze(2)
                                          .to_broadcast([P, PARTS, NK, QUAD]),
                                          ALU.mult).then_inc(hotg_ready, 1)
                        dve.wait_ge(hotg_ready, b * QB + q + 1)

            @block.tensor
            def _(pe):
                pe.sem_inc(quad_done, 2)

                def chunk(j, group):
                    n = U0 + j
                    pe.wait_ge(lo_done, group + n + 1)
                    pe.wait_ge(z_free, group + j + 1)
                    unit_product(bank[j % 2][:, :], n, act).then_inc(unit_used, 1)

                for j in range(HEAD_CHUNKS):
                    chunk(j, 0)
                with pe.Fori(0, NT // 2) as pair:
                    for s in range(2):
                        for j in range(TILE_CHUNKS):
                            chunk(HEAD_CHUNKS + s * TILE_CHUNKS + j, pair * PAIR_CHUNKS)
                        pe.wait_ge(tk_slots, pair * 2 + s + 1)
                        for a in range(3):
                            ins = nc.tensor.transpose(bank[2][:, a * P:(a + 1) * P],
                                                      slot[:, a, :, :].rearrange("p h k -> p (h k)"), ident)
                        ins.then_inc(tk_tr, 1)
                base = HEAD_CHUNKS + 2 * PAIR_CHUNKS
                with pe.Fori(0, GATE_BODIES) as b:
                    for j in range(BLOCK_CHUNKS):
                        chunk(base + j, b * BLOCK_CHUNKS)
                        for q in (2 * j, 2 * j + 1):
                            pe.wait_ge(hotg_ready, b * QB + q + 1)
                            pe.wait_ge(quad_out, b * QB + q + 1)
                            for t in range(QUAD):
                                for g in range(PARTS):
                                    ins = nc.tensor.matmul(bank[4 + q % 4][:, t * P:(t + 1) * P],
                                                           hot[:, q % 2, 0, :, t], hotg[:, q % 2, g, :, t],
                                                           start=g == 0, stop=g == PARTS - 1)
                            ins.then_inc(quad_done, 1)
                base += GATE_BODIES * BLOCK_CHUNKS
                for j in range(NC - base):
                    chunk(base + j, 0)

        ctx = ExitStack()
        with ctx:
            fnb = sb(ctx, "fnb", [P, 2, T])
            fpair = sb(ctx, "fpair", [P, 3, T])
            fsq = sb(ctx, "fsq", [P, KD, T])
            aw = sb(ctx, "aw", [P, 2, T])
            aws = sb(ctx, "aws", [P, 2, 4, T], F32R)

            a_mult, a_hi, a_lo = sem("a_mult"), sem("a_hi"), sem("a_lo")
            bank_final = sem("bank_final")
            f_h, f_sq, f_ms, f_mean, f_root, f_inv, f_out, stored = (
                sem("f_h"), sem("f_sq"), sem("f_ms"), sem("f_mean"), sem("f_root"), sem("f_inv"),
                sem("f_out"), sem("stored"))
            f_pair = sem("f_pair")
            BODY = 8
            BODIES = NC // BODY

            block = ctx.enter_context(nc.Block())

            @block.sync
            def _(sp):
                def body(g, units):
                    for half in range(2):
                        for j in range(4):
                            n = V0 + LOAD_LEAD + 4 * half + j
                            if 4 * half + j < units:
                                sp.wait_ge(lo_done, g * BODY + n - RAW + 1)
                                sp.dma_start(raw[:, n % RAW, :], v_tab[:, g * BODY + (n - V0), :]) \
                                    .then_inc(unit_loaded[n % RAW], 16)
                        if units == BODY:
                            sp.wait_ge(a_mult, g * BODY + 4 * half + 4)
                            mix(sp, half, g * 2 + half + 2)

                for slot_no in range(4):
                    sp.wait_ge(gelu_stored[slot_no], 16 * (NC // 4 + 1))
                with sp.Fori(0, BODIES - 1) as g:
                    body(g, BODY)
                body(BODIES - 1, BODY - LOAD_LEAD)
                for c in range(KD):
                    sp.wait_ge(f_out, c + 1)
                    sp.dma_start(yT[c * P:(c + 1) * P, :], ab[:, c, :]).then_inc(stored, 16)
                sp.wait_ge(stored, 16 * KD)

            @block.gpsimd
            def _(pool):
                with pool.Fori(0, BODIES - 1) as g:
                    for j in range(BODY):
                        split_lo(pool, V0 + LEAD + j, g * BODY)
                for j in range(BODY - LEAD):
                    split_lo(pool, V0 + LEAD + j, (BODIES - 1) * BODY)
                for i in range(3):
                    pool.wait_ge(f_sq, 2 * i + 2)
                    pool.tensor_tensor(fpair[:, i, :], fsq[:, 2 * i, :], fsq[:, 2 * i + 1, :], ALU.add) \
                        .then_inc(f_pair, 1)

            @block.scalar
            def _(act_e):
                def body(g, units):
                    for j in range(BODY):
                        act_e.wait_ge(a_mult, g * BODY + j + 1)
                        act_e.wait_ge(unit_used, g * BODY + (V0 + j - 3))
                        act_e.activation(aws[:, 0, j % 4, :], aw[:, j % 2, :], ACT.Copy).then_inc(a_hi, 1)
                        if j < units:
                            split_hi(act_e, V0 + LEAD + j, g * BODY)

                with act_e.Fori(0, BODIES - 1) as g:
                    body(g, BODY)
                body(BODIES - 1, BODY - LEAD)
                for c in range(KD):
                    act_e.wait_ge(f_h, c + 1)
                    act_e.activation(fsq[:, c, :], ab[:, c, :], ACT.Square).then_inc(f_sq, 1)
                act_e.wait_ge(f_mean, 1)
                act_e.activation(fnb[:, 1, :], fnb[:, 0, :], ACT.Sqrt).then_inc(f_root, 1)

            @block.vector
            def _(dve):
                def body(g):
                    for j in range(BODY):
                        half = j // 4
                        if j % 4 == 0:
                            dve.wait_ge(mix_in[half], g * 32 + 32)
                        dve.tensor_tensor(aw[:, j % 2, :].rearrange("p (b t) -> p b t", t=TB),
                                          gelu_in[:, half, j % 4, :].rearrange("p (b t) -> p b t", t=TB),
                                          gates_in[:, half, :, j % 4, :], ALU.mult).then_inc(a_mult, 1)
                        dve.wait_ge(a_hi, g * BODY + j + 1)
                        dve.tensor_tensor(aws[:, 1, j % 4, :], aw[:, j % 2, :],
                                          aws[:, 0, j % 4, :].bitcast(F32), ALU.subtract).then_inc(a_lo, 1)
                        dve.wait_ge(a_lo, g * BODY + j + 1)

                with dve.Fori(0, BODIES) as g:
                    body(g)
                for c in range(KD):
                    dve.wait_ge(bank_final, c + 1)
                    dve.tensor_tensor(ab[:, c, :], bank[c][:, :], ab[:, c, :], ALU.add).then_inc(f_h, 1)
                dve.wait_ge(f_ms, 5)
                dve.tensor_scalar(fnb[:, 0, :], bank[0][:, :], 1.0 / D, EPS, ALU.mult, ALU.add).then_inc(f_mean, 1)
                dve.wait_ge(f_root, 1)
                dve.reciprocal(fnb[:, 0, :], fnb[:, 1, :]).then_inc(f_inv, 1)
                dve.wait_ge(f_inv, 1)
                for c in range(KD):
                    dve.scalar_tensor_tensor(out=ab[:, c, :], in0=ab[:, c, :], scalar=nrm[:, 2, c:c + 1],
                                             in1=fnb[:, 0, :], op0=ALU.mult, op1=ALU.mult).then_inc(f_out, 1)

            @block.tensor
            def _(pe):
                def mean_square(i):
                    pe.wait_ge(f_pair if i < 3 else f_sq, i + 1 if i < 3 else i + 4)
                    x = fpair[:, i, :] if i < 3 else fsq[:, i + 3, :]
                    nc.tensor.matmul(bank[0][:, :], ones, x, start=i == 0, stop=i == 4).then_inc(f_ms, 1)

                def body(g, first, last):
                    for j in range(BODY):
                        n = V0 + j
                        pe.wait_ge(lo_done, g * BODY + n + 1)
                        pe.wait_ge(a_lo, g * BODY + j + 1)
                        for d in range(KD):
                            c = slice(d * P, (d + 1) * P)
                            ins = passes(bank[d][:, :], spl[:, 0, n % SPL, c], spl[:, 1, n % SPL, c],
                                         aws[:, 0, j % 4, :], aws[:, 1, j % 4, :],
                                         first and j == 0, last and j == BODY - 1)
                            if last and j == BODY - 1:
                                ins.then_inc(bank_final, 1)
                                ins = None
                                if d >= 5:
                                    mean_square(d - 5)
                        if ins:
                            ins.then_inc(unit_used, 1)

                body(0, True, False)
                with pe.Fori(1, BODIES - 1) as g:
                    body(g, False, False)
                body(BODIES - 1, False, True)
                mean_square(3)
                mean_square(4)


def kernel(x, norm_mix_w, w_in, hgrn_lb_logits, hgrn_norm_w, fox_f_bias, w_branch_hgrn, w_branch_fox,
           w_out, norm_ffn_w, peer_w_q, peer_sub_keys, peer_u, peer_v, norm_final_w):
    import numpy as np
    import concourse.bacc as bacc
    from concourse.bass_utils import run_bass_kernel_spmd

    c = np.ascontiguousarray
    f = [np.asarray(a) for a in (x, norm_mix_w, w_in, hgrn_lb_logits, hgrn_norm_w, fox_f_bias,
                                 w_branch_hgrn, w_branch_fox, w_out, norm_ffn_w, peer_w_q,
                                 peer_sub_keys, peer_u, peer_v, norm_final_w)]
    (x, norm_mix_w, w_in, hgrn_lb_logits, hgrn_norm_w, fox_f_bias, w_branch_hgrn, w_branch_fox,
     w_out, norm_ffn_w, peer_w_q, peer_sub_keys, peer_u, peer_v, norm_final_w) = f

    s, t = np.meshgrid(np.arange(P), np.arange(P), indexing="ij")
    c_f32 = np.stack([np.eye(P), np.where(t > s, LOWEST / 3, 0.0), np.ones((P, P))], axis=1)
    masks = []
    for l in range(LEVELS):
        hs = 64 >> l
        masks.append((s // (2 * hs) == t // (2 * hs)) & (s % (2 * hs) < hs) & (t % (2 * hs) >= hs))
    masks.append(s == t)

    arrays = {
        "xT": c(x[0].T),
        "w_in": c(w_in[0]),
        "norm_mix": c(norm_mix_w[0].reshape(KD, P).T),
        "lb_logits": c(hgrn_lb_logits.reshape(2, HH, P).transpose(2, 0, 1)),
        "hgrn_norm": c(hgrn_norm_w[0].reshape(HH, P).T),
        "fox_bias": c(fox_f_bias[0].reshape(HF, 1)),
        "w_a": c(w_branch_hgrn[0]),
        "w_b": c(w_branch_fox[0]),
        "w_out": c(w_out[0]),
        "norm_ffn": c(norm_ffn_w[0].reshape(KD, P).T),
        "w_q": c(peer_w_q[0]),
        "keys": c(peer_sub_keys[0].reshape(NQ, NK, P).transpose(2, 0, 1)),
        "u_t": c(peer_u[0].reshape(NK, NC, KD, P).transpose(1, 3, 2, 0).reshape(NC, P, W)),
        "v_tab": c(peer_v[0].reshape(NK, NC, D)),
        "norm_final": c(norm_final_w.reshape(KD, P).T),
        "c_f32": c_f32.astype(np.float32),
        "c_mask": c(np.stack(masks, axis=1).reshape(P, 8 * P).astype(np.float32)),
        "c_iota": c(np.broadcast_to(np.arange(P, dtype=np.float32), (P, P))),
    }
    nc = bacc.Bacc("TRN2", target_bir_lowering=False, num_devices=1)
    args = {n: nc.dram_tensor("in_" + n, a.shape, mybir.dt.from_np(a.dtype), kind="ExternalInput").ap()
            for n, a in arrays.items()}
    y = nc.dram_tensor("out_yT", (D, T), F32, kind="ExternalOutput").ap()
    build(nc, yT=y, **args)
    r = run_bass_kernel_spmd(nc, [{"in_" + n: a for n, a in arrays.items()}], core_ids=[0])
    return c(np.asarray(r.results[0]["out_yT"]).T)[None]
```
